# Optimizing a Trainium2 kernel written in Bass

```python
import math
import jax, jax.numpy as jnp
from jax import lax
import numpy as np

D_MODEL = 1024
BATCH = 1
SEQ = 1024
DEPTH = 1

N_META = 16
D_RNN = 1280
LRU_BLOCKS = 10
LRU_BLOCK = D_RNN // LRU_BLOCKS
CONV_WIDTH = 4
LRU_C = 8.0
N_HEADS = 8
HEAD_DIM = 128
KV_RANK = 256
IDX_HEADS = 8
IDX_DIM = 64
TOPK_MAX = 256
Q_BLOCK = 128
D_FF = 4 * D_MODEL
DEEPNORM_ALPHA = (2.0 * DEPTH) ** 0.25
DEEPNORM_BETA = (8.0 * DEPTH) ** -0.25
LN_EPS = 1e-5
NEG_INF = -1e30
IN_SPLITS = (D_RNN, D_RNN, N_HEADS * HEAD_DIM, KV_RANK, IDX_HEADS * IDX_DIM, IDX_DIM, IDX_HEADS, D_MODEL, D_MODEL)
D_IN = sum(IN_SPLITS)

kernel_name = "hybrid_rglru_dsa_gated_deepnorm"

def layer_norm(x, g, b):
    xf = x.astype(jnp.float32)
    mu = jnp.mean(xf, axis=-1, keepdims=True)
    var = jnp.mean(jnp.square(xf - mu), axis=-1, keepdims=True)
    return ((xf - mu) * lax.rsqrt(var + LN_EPS) * g.astype(jnp.float32) + b.astype(jnp.float32)).astype(x.dtype)

def unit_layer_norm(x):
    xf = x.astype(jnp.float32)
    mu = jnp.mean(xf, axis=-1, keepdims=True)
    var = jnp.mean(jnp.square(xf - mu), axis=-1, keepdims=True)
    return ((xf - mu) * lax.rsqrt(var + LN_EPS)).astype(x.dtype)

def rms_norm(x, g):
    xf = x.astype(jnp.float32)
    ms = jnp.mean(jnp.square(xf), axis=-1, keepdims=True)
    return (xf * lax.rsqrt(ms + LN_EPS) * g.astype(jnp.float32)).astype(x.dtype)

def split_columns(proj):
    offsets = []
    acc = 0
    for w in IN_SPLITS[:-1]:
        acc += w
        offsets.append(acc)
    return jnp.split(proj, offsets, axis=-1)

def causal_depthwise_conv(x, w, b):
    y = lax.conv_general_dilated(
        x, w[:, None, :], window_strides=(1,), padding=[(CONV_WIDTH - 1, 0)],
        dimension_numbers=('NWC', 'WIO', 'NWC'), feature_group_count=x.shape[-1])
    return y + b

def block_diag_linear(x, w, b):
    B, T, _ = x.shape
    xb = x.reshape(B, T, LRU_BLOCKS, LRU_BLOCK)
    return jnp.einsum('btnc,ncd->btnd', xb, w).reshape(B, T, D_RNN) + b

def rg_lru(x, w_a, b_a, w_x, b_x, lam):
    r = jax.nn.sigmoid(block_diag_linear(x, w_a, b_a)).astype(jnp.float32)
    i = jax.nn.sigmoid(block_diag_linear(x, w_x, b_x)).astype(jnp.float32)
    log_a = -LRU_C * r * jax.nn.softplus(-lam.astype(jnp.float32))
    a = jnp.exp(log_a)
    u = jnp.sqrt(-jnp.expm1(2.0 * log_a)) * (i * x.astype(jnp.float32))

    def combine(left, right):
        a1, b1 = left
        a2, b2 = right
        return a1 * a2, a2 * b1 + b2

    _, h = lax.associative_scan(combine, (a, u), axis=1)
    return h.astype(x.dtype)

def recurrent_branch(x_lru, g_lru, conv_w, conv_b, w_rg_a, b_rg_a, w_rg_x, b_rg_x, lam, w_branch):
    xc = causal_depthwise_conv(x_lru, conv_w, conv_b)
    h = rg_lru(xc, w_rg_a, b_rg_a, w_rg_x, b_rg_x, lam)
    return (h * jax.nn.gelu(g_lru)) @ w_branch

def sparse_attention(q, c_kv, q_idx, k_idx, w_idx, w_uk, w_uv, k_top):
    B, T = q.shape[0], q.shape[1]
    q_abs = jnp.einsum('bthd,hrd->bthr', q, w_uk)
    n_blk = -(-T // Q_BLOCK)
    Tp = n_blk * Q_BLOCK
    pad = Tp - T

    def to_blocks(a):
        a = jnp.pad(a, [(0, 0), (0, pad)] + [(0, 0)] * (a.ndim - 2))
        return jnp.moveaxis(a.reshape((B, n_blk, Q_BLOCK) + a.shape[2:]), 1, 0)

    q_pos = jnp.arange(Tp, dtype=jnp.int32).reshape(n_blk, Q_BLOCK)
    key_pos = jnp.arange(T, dtype=jnp.int32)
    batch_idx = jnp.arange(B, dtype=jnp.int32)[:, None, None]
    scale = HEAD_DIM ** -0.5

    def one_block(args):
        qa, qi, wi, qpos = args
        logits = jnp.einsum('bqhd,bsd->bqhs', qi, k_idx)
        score = jnp.einsum('bqh,bqhs->bqs', wi, jax.nn.relu(logits)).astype(jnp.float32)
        causal = key_pos[None, :] <= qpos[:, None]
        score = jnp.where(causal[None], score, NEG_INF)
        _, idx = lax.top_k(score, k_top)
        valid = idx <= qpos[None, :, None]
        c_sel = c_kv[batch_idx, idx]
        s = jnp.einsum('bqhr,bqkr->bqhk', qa, c_sel).astype(jnp.float32) * scale
        s = jnp.where(valid[:, :, None, :], s, NEG_INF)
        p = jax.nn.softmax(s, axis=-1).astype(c_kv.dtype)
        return jnp.einsum('bqhk,bqkr->bqhr', p, c_sel)

    o_lat = lax.map(one_block, (to_blocks(q_abs), to_blocks(q_idx), to_blocks(w_idx), q_pos))
    o_lat = jnp.moveaxis(o_lat, 0, 1).reshape(B, Tp, N_HEADS, KV_RANK)[:, :T]
    o = jnp.einsum('bthr,hrd->bthd', o_lat, w_uv)
    return o.reshape(B, T, N_HEADS * HEAD_DIM)

def hybrid_layer(x, k_top, w_in, conv_w, conv_b, w_rg_a, b_rg_a, w_rg_x, b_rg_x, lam, kv_norm_g,
                 w_uk, w_uv, w_branch_a, w_branch_b, w_out, ln1_g, ln1_b,
                 w_up, b_up, w_down, b_down, ln2_g, ln2_b):
    B, T, _ = x.shape
    proj = x @ w_in
    x_lru, g_lru, q, c_kv, q_idx, k_idx, w_idx, gate_a, gate_b = split_columns(proj)

    y_a = recurrent_branch(x_lru, g_lru, conv_w, conv_b, w_rg_a, b_rg_a, w_rg_x, b_rg_x, lam, w_branch_a)

    q = q.reshape(B, T, N_HEADS, HEAD_DIM)
    c_kv = rms_norm(c_kv, kv_norm_g)
    q_idx = q_idx.reshape(B, T, IDX_HEADS, IDX_DIM)
    k_idx = unit_layer_norm(k_idx)
    w_idx = w_idx * (IDX_HEADS ** -0.5 * IDX_DIM ** -0.5)
    y_b = sparse_attention(q, c_kv, q_idx, k_idx, w_idx, w_uk, w_uv, k_top) @ w_branch_b

    mixed = jax.nn.sigmoid(gate_a) * y_a + jax.nn.sigmoid(gate_b) * y_b
    x = layer_norm(DEEPNORM_ALPHA * x + mixed @ w_out, ln1_g, ln1_b)

    h = jnp.square(jax.nn.relu(x @ w_up + b_up))
    x = layer_norm(DEEPNORM_ALPHA * x + (h @ w_down + b_down), ln2_g, ln2_b)
    return x

def setup_inputs(seed: int = 0) -> dict:
    key = jax.random.key(seed)
    ks = jax.random.split(key, 32)
    f32 = jnp.float32

    def nrm(k, shape, scale):
        return jax.random.normal(k, shape, f32) * scale

    u = jax.random.uniform(ks[10], (DEPTH, D_RNN), f32, 0.9, 0.999)
    a0 = u ** (1.0 / LRU_C)
    lam = jnp.log(a0) - jnp.log1p(-a0)
    return {
        "x": nrm(ks[0], (BATCH, SEQ, D_MODEL), 1.0),
        "meta_tokens": nrm(ks[1], (N_META, D_MODEL), 1.0),
        "ln_in_g": 1.0 + nrm(ks[2], (D_MODEL,), 0.02),
        "ln_in_b": nrm(ks[3], (D_MODEL,), 0.02),
        "w_in": nrm(ks[4], (DEPTH, D_MODEL, D_IN), D_MODEL ** -0.5),
        "conv_w": nrm(ks[5], (DEPTH, CONV_WIDTH, D_RNN), CONV_WIDTH ** -0.5),
        "conv_b": nrm(ks[6], (DEPTH, D_RNN), 0.02),
        "w_rg_a": nrm(ks[7], (DEPTH, LRU_BLOCKS, LRU_BLOCK, LRU_BLOCK), LRU_BLOCK ** -0.5),
        "b_rg_a": nrm(ks[8], (DEPTH, D_RNN), 0.02),
        "w_rg_x": nrm(ks[9], (DEPTH, LRU_BLOCKS, LRU_BLOCK, LRU_BLOCK), LRU_BLOCK ** -0.5),
        "b_rg_x": nrm(ks[11], (DEPTH, D_RNN), 0.02),
        "lru_lambda": lam,
        "kv_norm_g": 1.0 + nrm(ks[12], (DEPTH, KV_RANK), 0.02),
        "w_uk": nrm(ks[13], (DEPTH, N_HEADS, KV_RANK, HEAD_DIM), KV_RANK ** -0.5),
        "w_uv": nrm(ks[14], (DEPTH, N_HEADS, KV_RANK, HEAD_DIM), KV_RANK ** -0.5),
        "w_branch_a": nrm(ks[15], (DEPTH, D_RNN, D_MODEL), D_RNN ** -0.5),
        "w_branch_b": nrm(ks[16], (DEPTH, N_HEADS * HEAD_DIM, D_MODEL), (N_HEADS * HEAD_DIM) ** -0.5),
        "w_out": nrm(ks[17], (DEPTH, D_MODEL, D_MODEL), D_MODEL ** -0.5 * DEEPNORM_BETA),
        "ln1_g": 1.0 + nrm(ks[18], (DEPTH, D_MODEL), 0.02),
        "ln1_b": nrm(ks[19], (DEPTH, D_MODEL), 0.02),
        "w_up": nrm(ks[20], (DEPTH, D_MODEL, D_FF), D_MODEL ** -0.5),
        "b_up": nrm(ks[21], (DEPTH, D_FF), 0.02),
        "w_down": nrm(ks[22], (DEPTH, D_FF, D_MODEL), D_FF ** -0.5 * DEEPNORM_BETA),
        "b_down": nrm(ks[23], (DEPTH, D_MODEL), 0.02),
        "ln2_g": 1.0 + nrm(ks[24], (DEPTH, D_MODEL), 0.02),
        "ln2_b": nrm(ks[25], (DEPTH, D_MODEL), 0.02),
    }

def reference(x, meta_tokens, ln_in_g, ln_in_b, w_in, conv_w, conv_b, w_rg_a, b_rg_a, w_rg_x, b_rg_x,
              lru_lambda, kv_norm_g, w_uk, w_uv, w_branch_a, w_branch_b, w_out, ln1_g, ln1_b,
              w_up, b_up, w_down, b_down, ln2_g, ln2_b):
    B, S, _ = x.shape
    meta = jnp.broadcast_to(meta_tokens[None].astype(x.dtype), (B, N_META, D_MODEL))
    h = jnp.concatenate([meta, x], axis=1)
    T = S + N_META
    k_top = min(TOPK_MAX, T // 4)
    h = layer_norm(h, ln_in_g, ln_in_b)
    for l in range(DEPTH):
        h = hybrid_layer(h, k_top, w_in[l], conv_w[l], conv_b[l], w_rg_a[l], b_rg_a[l], w_rg_x[l], b_rg_x[l],
                         lru_lambda[l], kv_norm_g[l], w_uk[l], w_uv[l], w_branch_a[l], w_branch_b[l],
                         w_out[l], ln1_g[l], ln1_b[l], w_up[l], b_up[l], w_down[l], b_down[l],
                         ln2_g[l], ln2_b[l])
    return h[:, N_META:]


_drawn_inputs = setup_inputs


def setup_inputs(seed=0):
    import zlib

    import numpy as np

    out = dict(_drawn_inputs(seed))
    spreads = {}
    factors = {'meta_tokens': 3.285,
     'conv_b': 2.818,
     'b_rg_a': 200.0,
     'b_rg_x': 64.0,
     'kv_norm_g': 8.0,
     'ln1_g': 2.785,
     'ln1_b': 2.688,
     'b_up': 4.592,
     'b_down': 19.037,
     'ln2_g': 23.186,
     'ln2_b': 22.849,
     'w_rg_a': 3.266}
    for name, (base, spread) in spreads.items():
        noise = np.random.default_rng([zlib.crc32(name.encode()), seed]).standard_normal(out[name].shape)
        drawn = base * np.exp(spread * noise) if base else spread * noise
        out[name] = __import__('jax').numpy.asarray(drawn.astype(out[name].dtype))
    for name, factor in factors.items():
        out[name] = (out[name] * factor).astype(out[name].dtype)
    return out
```

```python
from contextlib import ExitStack

import concourse.bass as bass
from concourse import mybir

F32 = mybir.dt.float32
F32R = mybir.dt.float32r
I32 = mybir.dt.int32
BF16 = mybir.dt.bfloat16
ALU = mybir.AluOpType
ACT = mybir.ActivationFunctionType
AX_X = mybir.AxisListType.X

P = 128
D = 1024
KC = D // P
S = 1024
META = 16
T = S + META
NT = S // P
D_RNN = 1280
NB = D_RNN // P
HEADS = 8
RANK = 256
RC = RANK // P
IDX_HEADS = 8
IDX_DIM = 64
N_KW = IDX_DIM + IDX_HEADS
TOPK = 256
D_FF = 4096
NF = D_FF // P
EPS = 1e-5
NEG = -1e30
ALPHA = 2.0 ** 0.25
SCALE = float(P) ** -0.5
IDX_SCALE = IDX_HEADS ** -0.5 * IDX_DIM ** -0.5

N_PROJ = 2 * NB + 3 * KC
X_LRU, G_LRU, Q_T, GATE_A, GATE_B = 0, NB, 2 * NB, 2 * NB + KC, 2 * NB + 2 * KC
N_KVQ = RC + IDX_HEADS * IDX_DIM // P + 1

PASSES = ((0, 0), (0, 1), (1, 0))
KEYS = [META + P * (i + 1) for i in range(NT)]
SC_OFF = [0] * NT
for _i in range(2, NT):
    SC_OFF[_i] = SC_OFF[_i - 1] + KEYS[_i - 1]
SC_LEN = SC_OFF[-1] + KEYS[-1]
MB_OFF = [sum(KEYS[:i]) for i in range(NT)]
MB_LEN = sum(KEYS)


def pieces(n, most=512):
    k = -(-n // most)
    w = -(-n // (2 * k)) * 2
    out, at = [], 0
    while at < n:
        out.append((at, min(w, n - at)))
        at += w
    return out


TOK3 = pieces(T)


def key_chunk(j):
    return (0, META) if j == 0 else (META + P * (j - 1), P)


def f32(ap):
    return ap.bitcast(F32)


class Kit:

    spent = []

    def __init__(self, nc, stage):
        self.nc, self.stage, self.ctx = nc, stage, ExitStack()

    def __enter__(self):
        self.ctx.__enter__()
        return self

    def __exit__(self, *a):
        return self.ctx.__exit__(*a)

    def sb(self, name, shape, dt=F32):
        return self.ctx.enter_context(self.nc.sbuf_tensor(f"{self.stage}_{name}", shape, dt))

    def ps(self, name, shape, dt=F32):
        return self.ctx.enter_context(self.nc.psum_tensor(f"{self.stage}_{name}", shape, dt))

    def sem(self, name):
        self.spent.append(self.nc.alloc_semaphore(name=f"{self.stage}_{name}"))
        return self.spent[-1]

    def block(self):
        return self.ctx.enter_context(self.nc.Block())


def recycle(nc):
    nc.clear_and_free_semaphores(Kit.spent)
    nc.all_engine_barrier()
    Kit.spent.clear()


def refine_rsqrt(dve, var, sd, rs, tmp):
    dve.reciprocal(rs, sd)
    dve.drain()
    dve.scalar_tensor_tensor(out=tmp, in0=rs, scalar=rs, in1=var, op0=ALU.mult, op1=ALU.mult)
    dve.drain()
    dve.tensor_scalar(tmp, tmp, -0.5, 1.5, ALU.mult, ALU.add)
    dve.drain()
    dve.tensor_tensor(rs, rs, tmp, ALU.mult)
    dve.drain()


def stage_norm(nc, io, hT):
    with Kit(nc, "ln0") as k:
        sources = [io["meta_tokens"]] + [io["x"][P * t:P * t + P, :] for t in range(NT)]
        N = NT + 1
        rows = [META] + [P] * NT
        cols = [sum(rows[:t]) for t in range(N)]
        xin = k.sb("xin", [P, 3, D])
        hn = k.sb("hn", [P, 2, D])
        gain, shift = k.sb("gain", [P, D]), k.sb("shift", [P, D])
        ident = k.sb("ident", [P, P])
        stats = k.sb("stats", [P, 2, 6])
        mv = k.sb("mv", [P, 2])
        eps, var, sd, tmp = (k.sb(n, [P, 1]) for n in ("eps", "var", "sd", "tmp"))
        scale, bias = k.sb("scale", [P, N]), k.sb("bias", [P, N])
        psT = k.ps("psT", [P, 4, 512])
        (gain_loaded, shift_loaded, id0, id_ready, var_ready, sd_ready, scale_ready, normed, gained, h_ready,
         transposed, high, low) = (k.sem(n) for n in (
             "gain_loaded", "shift_loaded", "id0", "id_ready", "var_ready", "sd_ready", "scale_ready", "normed",
             "gained", "h_ready", "transposed", "high", "low"))
        loaded = [k.sem(f"loaded{b}") for b in range(3)]
        stored = [k.sem("stored0"), k.sem("stored1")]
        block = k.block()

        def psum_of(t):
            return psT[:, 2 * (t % 2):2 * (t % 2) + 2, :].rearrange("p b (c n) -> p (b c) n", c=4)[:, :, 0:rows[t]]

        def columns(t):
            return slice(cols[t], cols[t] + rows[t])

        def stores(t, s):
            return len([i for i in range(1, t + 1) if i % 2 == s])

        @block.sync
        def _(sp):
            def store(t):
                sp.wait_ge(h_ready, t + 1)
                sp.dma_start(io["h_tok"][t - 1], hn[:, t % 2, :]).then_inc(stored[t % 2], 16)

            for t in range(N):
                if t >= 3:
                    sp.wait_ge(normed, t - 2)
                sp.dma_start(xin[0:rows[t], t % 3, :], sources[t]).then_inc(loaded[t % 3], 16)
                if t == 1:
                    sp.dma_start(gain[:, :], io["ln_in_g"].partition_broadcast(P)).then_inc(gain_loaded, 16)
                    sp.dma_start(shift[:, :], io["ln_in_b"].partition_broadcast(P)).then_inc(shift_loaded, 16)
                if t >= 4:
                    store(t - 3)
            for t in range(N - 3, N):
                store(t)
            for s in range(2):
                sp.wait_ge(stored[s], 16 * stores(NT, s))

        @block.gpsimd
        def _(pool):
            pool.memset(ident[:, :], 0.0).then_inc(id0, 1)
            pool.wait_ge(id0, 1)
            pool.affine_select(out=ident[:, :], in_=ident[:, :], compare_op=ALU.not_equal, fill=1.0,
                               base=0, pattern=[[-1, P]], channel_multiplier=1).then_inc(id_ready, 1)
            pool.wait_ge(gain_loaded, 16)
            for t in range(N):
                n, s = rows[t], t % 2
                pool.wait_ge(normed, t + 1)
                pool.tensor_tensor(hn[0:n, s, :], hn[0:n, s, :], gain[0:n, :], ALU.mult).then_inc(gained, 1)

        @block.vector
        def _(dve):
            dve.memset(eps[:, :], EPS)
            dve.drain()

            def statistics(t):
                s, n = t % 3, rows[t]
                dve.wait_ge(loaded[s], 16 * (t // 3 + 1))
                for c in range(2):
                    dve.bn_stats(stats[0:n, c, :], xin[0:n, s, 512 * c:512 * c + 512])
                dve.drain()
                dve.bn_aggr(mv[0:n, :], stats[0:n, :, :])
                dve.drain()
                dve.tensor_tensor(var[0:n, :], mv[0:n, 1:2], eps[0:n, :], ALU.add).then_inc(var_ready, 1)

            def scale_and_bias(t):
                n, c = rows[t], slice(t, t + 1)
                dve.wait_ge(sd_ready, t + 1)
                refine_rsqrt(dve, var[0:n, :], sd[0:n, :], scale[0:n, c], tmp[0:n, :])
                dve.scalar_tensor_tensor(out=bias[0:n, c], in0=mv[0:n, 0:1], scalar=-1.0, in1=scale[0:n, c],
                                         op0=ALU.mult, op1=ALU.mult).then_inc(scale_ready, 1)
                dve.drain()

            def shift_tile(t):
                n, s = rows[t], t % 2
                dve.wait_ge(gained, t + 1)
                dve.tensor_tensor(hn[0:n, s, :], hn[0:n, s, :], shift[0:n, :], ALU.add).then_inc(h_ready, 1)

            def split_low(t):
                dve.wait_ge(high, t + 1)
                dve.tensor_tensor(hT[1][:, :, columns(t)], psum_of(t), f32(hT[0][:, :, columns(t)]),
                                  ALU.subtract).then_inc(low, 1)

            dve.wait_ge(shift_loaded, 16)
            for t in range(N + 2):
                if t < N:
                    statistics(t)
                if 1 <= t <= N:
                    shift_tile(t - 1)
                if t < N:
                    scale_and_bias(t)
                if t >= 2:
                    split_low(t - 2)

        @block.tensor
        def _(pe):
            pe.wait_ge(id_ready, 1)
            for t in range(N):
                pe.wait_ge(h_ready, t + 1)
                if t >= 2:
                    pe.wait_ge(low, t - 1)
                n = rows[t]
                for c in range(KC):
                    last = pe.transpose(psum_of(t)[:, c, :], hn[0:n, t % 2, P * c:P * c + P], ident[0:n, 0:n])
                last.then_inc(transposed, 1)

        @block.scalar
        def _(act):
            def root(t):
                n = rows[t]
                act.wait_ge(var_ready, t + 1)
                act.activation(sd[0:n, :], var[0:n, :], ACT.Sqrt).then_inc(sd_ready, 1)

            def normalise(t):
                n, s = rows[t], t % 2
                act.wait_ge(scale_ready, t + 1)
                if t >= 2:
                    act.wait_ge(transposed, t - 1)
                    if stores(t - 2, s):
                        act.wait_ge(stored[s], 16 * stores(t - 2, s))
                act.activation(hn[0:n, s, :], xin[0:n, t % 3, :], ACT.Identity, bias=bias[0:n, t:t + 1],
                               scale=scale[0:n, t:t + 1]).then_inc(normed, 1)

            def split_high(t):
                act.wait_ge(transposed, t + 1)
                act.activation(hT[0][:, :, columns(t)], psum_of(t), ACT.Copy).then_inc(high, 1)

            for t in range(N + 1):
                if t < N:
                    root(t)
                    normalise(t)
                if t >= 1:
                    split_high(t - 1)


def stage_project(nc, k, hT, weights, n_tiles, out_of, store_to, extra_vector=None,
                  func_of=lambda t: ACT.Copy):
    raw = k.sb("raw", [P, 2, KC, P])
    w = [k.sb("w_high", [P, 2, KC, P], F32R), k.sb("w_low", [P, 2, KC, P], F32R)]
    ps = k.ps("ps", [P, 2, 3, 512])
    w_loaded = [k.sem("w_loaded0"), k.sem("w_loaded1")]
    w_high = k.sem("w_high_ready")
    w_low = k.sem("w_low_ready")
    mm_done = k.sem("mm_done")
    evicted = k.sem("evicted")
    stored = [k.sem("stored0"), k.sem("stored1")]
    block = k.block()
    bodies = n_tiles // 2

    @block.sync
    def _(sp):
        def body(j, first):
            for s in range(2):
                if not first:
                    sp.wait_ge(w_low, 2 * j + (s - 1))
                sp.dma_start(raw[:, s, :, :], weights[bass.ds(2 * j + s, 1)].rearrange("a p c n -> p (a c) n")
                             ).then_inc(w_loaded[s], 16)
        body(0, True)
        with sp.Fori(1, bodies) as j:
            body(j, False)
        if n_tiles % 2:
            sp.wait_ge(w_low, n_tiles - 2)
            sp.dma_start(raw[:, 0, :, :], weights[n_tiles - 1]).then_inc(w_loaded[0], 16)

    if store_to is not None:
        @block.gpsimd
        def _(pool):
            with pool.Fori(0, bodies) as j:
                for s in range(2):
                    pool.wait_ge(evicted, 2 * j + (s + 1))
                    pool.dma_start(store_to(2 * j + s), out_of(s, None)).then_inc(stored[s], 16)
            for s in range(2):
                pool.wait_ge(stored[s], 16 * bodies)

    @block.scalar
    def _(act):
        def split_high(j, s, first):
            act.wait_ge(w_loaded[s], 16 * j + 16)
            if not first:
                act.wait_ge(mm_done, 2 * j + (s - 1))
            act.activation(w[0][:, s], raw[:, s], ACT.Copy).then_inc(w_high, 1)

        def evict(t, s, stores_before, func):
            act.wait_ge(mm_done, t + 1)
            if store_to is not None and stores_before is not None:
                act.wait_ge(stored[s], 16 * stores_before)
            for c, (at, n) in enumerate(TOK3):
                last = act.activation(out_of(s, t)[:, at:at + n], ps[:, s, c, 0:n], func)
            last.then_inc(evicted, 1)

        split_high(0, 0, True)
        split_high(0, 1, True)
        evict(0, 0, None, func_of(0))
        split_high(1, 0, False)
        evict(1, 1, None, func_of(1))
        split_high(1, 1, False)
        evict(2, 0, 1, func_of(2))
        at = 2
        while at < bodies:
            end = at + 1
            while end < bodies and len({func_of(t) for t in range(2 * at - 1, 2 * end + 1)}) == 1:
                end += 1
            f1, f0 = func_of(2 * at - 1), func_of(2 * at)
            with act.Fori(at, end) as j:
                split_high(j, 0, False)
                evict(2 * j - 1, 1, j - 1, f1)
                split_high(j, 1, False)
                evict(2 * j, 0, j, f0)
            at = end
        if n_tiles % 2:
            split_high(bodies, 0, False)
        evict(2 * bodies - 1, 1, bodies - 1, func_of(2 * bodies - 1))
        if n_tiles % 2:
            evict(n_tiles - 1, 0, bodies, func_of(n_tiles - 1))

    @block.vector
    def _(dve):
        def split_low(t, s):
            dve.wait_ge(w_high, t + 1)
            dve.tensor_tensor(w[1][:, s], raw[:, s], f32(w[0][:, s]), ALU.subtract).then_inc(w_low, 1)
        if extra_vector is None:
            with dve.Fori(0, bodies) as j:
                for s in range(2):
                    split_low(2 * j + s, s)
            if n_tiles % 2:
                split_low(n_tiles - 1, 0)
        else:
            extra_vector(dve, split_low)

    @block.tensor
    def _(pe):
        def tile(t, s, first):
            pe.wait_ge(w_low, t + 1)
            if not first:
                pe.wait_ge(evicted, t - 1)
            for c in range(KC):
                for n_pass, (a, b) in enumerate(PASSES):
                    for q, (at, n) in enumerate(TOK3):
                        last = pe.matmul(ps[:, s, q, 0:n], w[a][:, s, c, :], hT[b][:, c, at:at + n],
                                         start=(c == 0 and n_pass == 0), stop=(c == KC - 1 and n_pass == 2))
            last.then_inc(mm_done, 1)
        tile(0, 0, True)
        tile(1, 1, True)
        with pe.Fori(1, bodies) as j:
            tile(2 * j, 0, False)
            tile(2 * j + 1, 1, False)
        if n_tiles % 2:
            tile(n_tiles - 1, 0, False)


def stage_project_kvq(nc, io, hT, kvq):
    with Kit(nc, "pkv") as k:
        stage_project(nc, k, hT, io["w_kvq"], N_KVQ,
                      lambda s, t: kvq[:, bass.ds(t, 1), :].rearrange("p a n -> p (a n)"), None)


def stage_keys(nc, io, kvq, ctok, cT, kT2, widx, qs):
    with Kit(nc, "keys") as k:
        ident = k.sb("ident", [P, P])
        g = k.sb("g", [P, RANK])
        eps = k.sb("eps", [P, 1])
        stats = k.sb("stats", [P, 6])
        mv = k.sb("mv", [P, NT + 1, 2])
        ms = k.sb("ms", [P, NT + 1])
        sq = k.sb("sq", [P, 2, RANK])
        sd = k.sb("sd", [P, NT + 1, 2])
        rs = k.sb("rs", [P, NT + 1, 2])
        tok = k.sb("tok", [P, 2, RANK + P])
        ps_in = k.ps("ps_in", [P, 2, 512])
        ps_out = k.ps("ps_out", [P, 2, 512])
        consts, id0, id_ready, eps_ready = (k.sem(x) for x in ("consts", "id0", "id_ready", "eps_ready"))
        t_in, sq_ready, var_ready, sd_ready, tok_ready, tok_high, tok_low, t_out, out_high, out_low = (
            k.sem(x) for x in ("t_in", "sq_ready", "var_ready", "sd_ready", "tok_ready", "tok_high", "tok_low",
                               "t_out", "out_high", "out_low"))
        q_high, q_low, stacked = k.sem("q_high"), k.sem("q_low"), k.sem("stacked")
        block = k.block()
        N = NT + 1

        def head_rows(h):
            return slice(IDX_DIM * (h % 2), IDX_DIM * (h % 2) + IDX_DIM)

        def head_queries(h):
            return kvq[head_rows(h), RC + h // 2, META:T]

        @block.sync
        def _(sp):
            sp.dma_start(g[:, :], io["kv_norm_g"].partition_broadcast(P)).then_inc(consts, 16)
            for h in range(IDX_HEADS):
                sp.wait_ge(q_low, h + 1)
                sp.dma_start(f32(qs[head_rows(h + 1), h, :]), head_queries(h)).then_inc(stacked, 16)
            sp.wait_ge(stacked, 16 * IDX_HEADS)

        @block.gpsimd
        def _(pool):
            pool.memset(ident[:, :], 0.0).then_inc(id0, 1)
            pool.wait_ge(id0, 1)
            pool.affine_select(out=ident[:, :], in_=ident[:, :], compare_op=ALU.not_equal, fill=1.0,
                               base=0, pattern=[[-1, P]], channel_multiplier=1).then_inc(id_ready, 1)

        @block.tensor
        def _(pe):
            pe.wait_ge(id_ready, 1)

            def back(j):
                at, n = key_chunk(j)
                pe.wait_ge(tok_ready, j + 1)
                if j >= 2:
                    pe.wait_ge(out_low, j - 1)
                for c in range(RC + 1):
                    last = pe.transpose(ps_out[:, j % 2, P * c:P * c + n], tok[0:n, j % 2, P * c:P * c + P],
                                        ident[0:n, 0:n])
                last.then_inc(t_out, 1)

            for j in range(N):
                at, n = key_chunk(j)
                if j >= 2:
                    pe.wait_ge(tok_ready, j - 1)
                for c in range(RC):
                    pe.transpose(ps_in[0:n, j % 2, P * c:P * c + P], kvq[:, c, at:at + n], ident[:, :])
                pe.transpose(ps_in[0:n, j % 2, RANK:RANK + N_KW], kvq[0:N_KW, N_KVQ - 1, at:at + n],
                             ident[0:N_KW, 0:N_KW]).then_inc(t_in, 1)
                if j >= 1:
                    back(j - 1)
            back(N - 1)

        @block.scalar
        def _(act):
            act.wait_ge(eps_ready, 1)

            def split_high(j):
                at, n = key_chunk(j)
                act.wait_ge(tok_ready, j + 1)
                act.activation(ctok[0][0:n, j, :], tok[0:n, j % 2, 0:RANK], ACT.Copy).then_inc(tok_high, 1)
                act.wait_ge(t_out, j + 1)
                act.activation(cT[0][:, :, at:at + n], ps_out[:, j % 2, 0:RANK].rearrange(
                    "p (c n) -> p c n", c=RC)[:, :, 0:n], ACT.Copy)
                act.activation(kT2[0][:, at:at + n], ps_out[:, j % 2, RANK:RANK + n], ACT.Copy).then_inc(out_high, 1)

            def mean_square(j):
                at, n = key_chunk(j)
                act.wait_ge(t_in, j + 1)
                act.activation(sq[0:n, j % 2, :], ps_in[0:n, j % 2, 0:RANK], ACT.Square, scale=RANK ** -0.5,
                               accum_out=ms[0:n, j:j + 1]).then_inc(sq_ready, 1)

            mean_square(0)
            for j in range(N):
                at, n = key_chunk(j)
                act.wait_ge(sq_ready, j + 1)
                act.wait_ge(var_ready, j + 1)
                act.activation(sd[0:n, j, 0:1], ms[0:n, j:j + 1], ACT.Sqrt, bias=eps[0:n, :])
                act.activation(sd[0:n, j, 1:2], mv[0:n, j, 1:2], ACT.Sqrt, bias=eps[0:n, :]).then_inc(sd_ready, 1)
                if j + 1 < N:
                    mean_square(j + 1)
                if j >= 1:
                    split_high(j - 1)
                if j < IDX_HEADS:
                    act.activation(qs[head_rows(j), j, :], head_queries(j), ACT.Copy).then_inc(q_high, 1)
            split_high(N - 1)

        @block.vector
        def _(dve):
            dve.memset(eps[:, :], EPS).then_inc(eps_ready, 1)
            dve.wait_ge(consts, 16)

            def split_low(j):
                at, n = key_chunk(j)
                dve.wait_ge(tok_high, j + 1)
                dve.tensor_tensor(ctok[1][0:n, j, :], tok[0:n, j % 2, 0:RANK], f32(ctok[0][0:n, j, :]),
                                  ALU.subtract).then_inc(tok_low, 1)
                dve.wait_ge(out_high, j + 1)
                dve.tensor_tensor(cT[1][:, :, at:at + n], ps_out[:, j % 2, 0:RANK].rearrange(
                    "p (c n) -> p c n", c=RC)[:, :, 0:n], f32(cT[0][:, :, at:at + n]), ALU.subtract)
                dve.tensor_tensor(kT2[1][:, at:at + n], ps_out[:, j % 2, RANK:RANK + n], f32(kT2[0][:, at:at + n]),
                                  ALU.subtract).then_inc(out_low, 1)

            def key_columns(j):
                return ps_in[0:key_chunk(j)[1], j % 2, RANK:RANK + IDX_DIM]

            def key_statistics(j):
                at, n = key_chunk(j)
                dve.wait_ge(sq_ready, j + 1)
                dve.bn_stats(stats[0:n, :], key_columns(j))
                dve.drain()
                dve.bn_aggr(mv[0:n, j, :], stats[0:n, :]).then_inc(var_ready, 1)
                dve.drain()

            key_statistics(0)
            for j in range(N):
                at, n = key_chunk(j)
                kcols = key_columns(j)
                dve.wait_ge(sd_ready, j + 1)
                dve.reciprocal(rs[0:n, j, :], sd[0:n, j, :])
                if j >= 1:
                    dve.tensor_scalar(widx[0:n, j - 1, :], ps_in[0:n, j % 2, RANK + IDX_DIM:RANK + N_KW], IDX_SCALE,
                                      None, ALU.mult)
                dve.drain()
                dve.scalar_tensor_tensor(out=tok[0:n, j % 2, 0:RANK], in0=ps_in[0:n, j % 2, 0:RANK],
                                         scalar=rs[0:n, j, 0:1], in1=g[0:n, :], op0=ALU.mult, op1=ALU.mult)
                dve.tensor_scalar(tok[0:n, j % 2, RANK:RANK + IDX_DIM], kcols, mv[0:n, j, 0:1], rs[0:n, j, 1:2],
                                  ALU.subtract, ALU.mult)
                dve.tensor_scalar(tok[0:n, j % 2, RANK + IDX_DIM:RANK + P], kcols, mv[0:n, j, 0:1], rs[0:n, j, 1:2],
                                  ALU.subtract, ALU.mult).then_inc(tok_ready, 1)
                if j + 1 < N:
                    key_statistics(j + 1)
                if j >= 1:
                    split_low(j - 1)
                if j < IDX_HEADS:
                    dve.wait_ge(q_high, j + 1)
                    dve.tensor_tensor(head_queries(j), head_queries(j), f32(qs[head_rows(j), j, :]),
                                      ALU.subtract).then_inc(q_low, 1)
            split_low(N - 1)


def stage_indexer(nc, qs, kT2, widx, scores):
    with Kit(nc, "idx") as k:
        relu = k.sb("relu", [P, 2, T])
        ps = k.ps("ps", [P, 2, 3, 512])
        logits, relu_ready, summed, tri = (k.sem(x) for x in ("logits", "relu_ready", "summed", "tri"))
        block = k.block()

        work = [(i, h) for i in range(1, NT) for h in range(IDX_HEADS)]

        @block.scalar
        def _(act):
            for n, (i, h) in enumerate(work):
                act.wait_ge(logits, n + 1)
                if n >= 2:
                    act.wait_ge(summed, n - 1)
                for q, (at, w) in enumerate(pieces(KEYS[i])):
                    last = act.activation(relu[:, n % 2, at:at + w], ps[:, n % 2, q, 0:w], ACT.Relu)
                last.then_inc(relu_ready, 1)

        @block.vector
        def _(dve):
            for n, (i, h) in enumerate(work):
                dve.wait_ge(relu_ready, n + 1)
                if n >= 1:
                    dve.wait_ge(summed, n)
                sc = scores[:, SC_OFF[i]:SC_OFF[i] + KEYS[i]]
                if h == 0:
                    dve.tensor_scalar(sc, relu[:, n % 2, 0:KEYS[i]], widx[:, i, 0:1], None,
                                      ALU.mult).then_inc(summed, 1)
                else:
                    dve.scalar_tensor_tensor(out=sc, in0=relu[:, n % 2, 0:KEYS[i]], scalar=widx[:, i, h:h + 1],
                                             in1=sc, op0=ALU.mult, op1=ALU.add).then_inc(summed, 1)

        @block.gpsimd
        def _(pool):
            for i in range(1, NT):
                pool.wait_ge(summed, IDX_HEADS * i)
                at = SC_OFF[i] + KEYS[i] - P
                pool.affine_select(out=scores[:, at:at + P], in_=scores[:, at:at + P], compare_op=ALU.is_ge,
                                   fill=NEG, base=0, pattern=[[-1, P]], channel_multiplier=1).then_inc(tri, 1)
            pool.wait_ge(tri, NT - 1)

        @block.tensor
        def _(pe):
            for n, (i, h) in enumerate(work):
                if n >= 2:
                    pe.wait_ge(relu_ready, n - 1)
                for part in range(2):
                    for q, (at, w) in enumerate(pieces(KEYS[i])):
                        last = pe.matmul(ps[:, n % 2, q, 0:w], qs[:, h, P * i:P * i + P],
                                         kT2[part][:, at:at + w], start=(part == 0), stop=(part == 1))
                last.then_inc(logits, 1)


N_SEL = NT - 1
FIRST_BIT_TILE = 2
FIRST_MASK_TILE = FIRST_BIT_TILE + 32


def tile_scores(scores, i):
    return scores[:, SC_OFF[i]:SC_OFF[i] + KEYS[i]]


def select_setup(dve, scores, sel, junk):
    for i in range(1, NT):
        dve.tensor_scalar(tile_scores(junk, i), tile_scores(scores, i), 0.0, 0.0, ALU.is_ge, ALU.add,
                          accum_out=sel["count"][:, i - 1:i])
        dve.memset(sel["rank_neg"][:, i - 1:i], float(KEYS[i] - TOPK + 1))
    dve.memset(sel["rank"][:, :], float(TOPK))
    dve.memset(sel["found"][:, :], 0)
    dve.memset(sel["bit"][:, :], 1 << 30)
    dve.drain()
    dve.tensor_scalar(sel["neg"][:, :], sel["count"][:, :], float(TOPK), None, ALU.is_lt)
    dve.drain()
    dve.copy_predicated(sel["rank"][:, :], sel["neg"][:, :], sel["rank_neg"][:, :])
    dve.tensor_scalar(sel["sign"][:, :], sel["count"][:, :], float(TOPK), None, ALU.is_ge)
    dve.drain()
    dve.tensor_scalar(sel["sign"][:, :], sel["sign"][:, :], 2.0, -1.0, ALU.mult, ALU.add)
    dve.drain()
    for i in range(1, NT):
        dve.tensor_scalar(tile_scores(scores, i), tile_scores(scores, i), sel["sign"][:, i - 1:i], None, ALU.mult)
    dve.drain()


def select_bit(dve, scores, sel, junk):
    dve.tensor_tensor(sel["cand"][:, :], sel["found"][:, :], sel["bit"][:, :], ALU.bitwise_or)
    dve.drain()
    for i in range(1, NT):
        dve.tensor_scalar(tile_scores(junk, i), tile_scores(scores, i), f32(sel["cand"][:, i - 1:i]), 0.0,
                          ALU.is_ge, ALU.add, accum_out=sel["count"][:, i - 1:i])
    dve.tensor_scalar(sel["bit"][:, :], sel["bit"][:, :], 1, None, ALU.logical_shift_right)
    dve.drain()
    dve.tensor_tensor(sel["more"][:, :], sel["count"][:, :], sel["rank"][:, :], ALU.is_ge)
    dve.drain()
    dve.copy_predicated(sel["found"][:, :], sel["more"][:, :], sel["cand"][:, :])
    dve.drain()


def select_mask(dve, i, scores, sel, work, maskb):
    n, c = KEYS[i], slice(i - 1, i)
    above, equal, order = (work[:, q, 0:n] for q in range(3))
    dve.tensor_tensor(sel["thr"][:, c], f32(sel["found"][:, c]), sel["sign"][:, c], ALU.mult)
    dve.tensor_scalar(tile_scores(scores, i), tile_scores(scores, i), sel["sign"][:, c], None, ALU.mult)
    dve.drain()
    dve.tensor_scalar(above, tile_scores(scores, i), sel["thr"][:, c], 0.0, ALU.is_gt, ALU.add,
                      accum_out=sel["count"][:, c])
    dve.tensor_scalar(equal, tile_scores(scores, i), sel["thr"][:, c], None, ALU.is_equal)
    dve.drain()
    dve.tensor_tensor_scan(order, equal, equal, 0.0, ALU.add, ALU.max)
    dve.tensor_scalar(sel["left"][:, c], sel["count"][:, c], -1.0, float(TOPK), ALU.mult, ALU.add)
    dve.drain()
    dve.scalar_tensor_tensor(out=equal, in0=order, scalar=sel["left"][:, c], in1=equal, op0=ALU.is_le,
                             op1=ALU.mult)
    dve.drain()
    dve.tensor_tensor(above, above, equal, ALU.add)
    dve.drain()
    dve.tensor_scalar(maskb[:, MB_OFF[i]:MB_OFF[i] + n], above, -1.0, -NEG, ALU.add, ALU.mult)
    dve.drain()


def stage_project_select(nc, io, hT, scores, maskb):
    with Kit(nc, "prj") as k:
        stage = k.sb("stage", [P, 2, T])
        work = k.sb("work", [P, 3, T])
        junk = k.sb("junk", [P, SC_LEN], BF16)
        sel = {n: k.sb(n, [P, N_SEL], I32 if n in ("found", "bit", "cand", "neg", "more") else F32)
               for n in ("count", "rank", "rank_neg", "sign", "thr", "left", "found", "bit", "cand", "neg", "more")}

        def vector_work(dve, split_low):
            for t in range(FIRST_BIT_TILE):
                split_low(t, t % 2)
            select_setup(dve, scores, sel, junk)
            with dve.Fori(FIRST_BIT_TILE // 2, FIRST_MASK_TILE // 2) as j:
                for s in range(2):
                    split_low(2 * j + s, s)
                    select_bit(dve, scores, sel, junk)
            for t in range(FIRST_MASK_TILE, N_PROJ):
                split_low(t, t % 2)
                i = t - FIRST_MASK_TILE + 1
                if i < NT:
                    select_mask(dve, i, scores, sel, work, maskb)

        stage_project(nc, k, hT, io["w_rest"], N_PROJ,
                      lambda s, t: stage[:, s, :],
                      lambda t: io["projT"][bass.ds(t, 1)].rearrange("a p n -> (a p) n"),
                      vector_work, lambda t: (ACT.Gelu_apprx_tanh if G_LRU <= t < Q_T else
                                              ACT.Sigmoid if t >= GATE_A else ACT.Copy))


GROUP = 2
GQ = GROUP * P
HG = 2
PAIRS = HEADS // HG
UNITS = [(i, h) for i in range(NT) for h in range(HEADS)]
GU = GROUP * HEADS


def score_pieces(n):
    k = 1 if n <= 512 else 2 if n <= 1024 else 4
    return [(n // k * q, n // k) for q in range(k)]


def transpose_steps(i):
    chunks = list(range(1, i + 2)) + [0]
    return [chunks[c:c + 4] for c in range(0, len(chunks), 4)]


def attention_jobs():
    at = {HG * w + 4: [("weigh", w)] for w in range(len(UNITS) // HG)}
    for g in range(NT // GROUP):
        for n, u in enumerate((3, 3, 5, 5)):
            at.setdefault(GU * (g + 1) + u, []).append(("expand", PAIRS * g + n))
        if g >= 1:
            for n, u in enumerate((7, 9, 11, 13)):
                at.setdefault(GU * (g - 1) + u, []).extend(
                    ("absorb", HEADS * g + h) for h in range(HG * n, HG * n + HG))
    return at


def stage_attention(nc, io, ctok, cT, maskb):
    with Kit(nc, "att") as k:
        U = len(UNITS)
        lat = [k.sb("lat_high", [P, 2, RC * HEADS, GQ], F32R), k.sb("lat_low", [P, 2, RC * HEADS, GQ], F32R)]
        wuk = [k.sb("wuk_high", [P, HEADS * RANK], F32R), k.sb("wuk_low", [P, HEADS * RANK], F32R)]
        wuv = [k.sb("wuv_high", [P, HEADS * RANK], F32R), k.sb("wuv_low", [P, HEADS * RANK], F32R)]
        ident = k.sb("ident", [P, P])
        masked = k.sb("masked", [P, 2, T])
        prob = k.sb("prob", [P, 3, T])
        pT = [k.sb("pT_high", [P, 2, NT + 1, HG, P], F32R), k.sb("pT_low", [P, 2, NT + 1, HG, P], F32R)]
        qraw = k.sb("qraw", [P, HG, GQ])
        q = [k.sb("q_high", [P, HG, GQ], F32R), k.sb("q_low", [P, HG, GQ], F32R)]
        out = k.sb("out", [P, 2, HG, GQ])
        top, bias, total, inv = (k.sb(x, [P, U]) for x in ("top", "bias", "total", "inv"))
        wraw = [m[:, 0:2, :].rearrange("p a n -> p (a n)")[:, 0:HEADS * RANK] for m in (masked, prob)]
        q_first = [m[:, :, :, :, :].rearrange("p s j h n -> p (s j h n)")[:, 0:HEADS * GQ].rearrange(
            "p (h n) -> p h n", n=GQ) for m in pT]
        ps_s = k.ps("ps_s", [P, 4, 512])
        ps_t = k.ps("ps_t", [P, 2, 4, P])
        ps_o = k.ps("ps_o", [P, 2, 512])
        (id0, id_ready, causal, w_high, w_low, q_first_loaded, q_loaded, q_high, q_low, scored, mask_added, biased,
         exped, normed,
         turned, t_high, t_low, job_done, o_high, o_low, expanded) = (k.sem(x) for x in (
             "id0", "id_ready", "causal", "w_high", "w_low", "q_first_loaded", "q_loaded", "q_high", "q_low", "scored",
             "mask_added",
             "biased", "exped", "normed", "turned", "t_high", "t_low", "job_done", "o_high", "o_low", "expanded"))
        w_loaded = [k.sem(f"w_loaded{n}") for n in range(3)]
        stored = [k.sem("stored0"), k.sem("stored1")]
        block = k.block()

        job_at = attention_jobs()
        jobs = [("absorb", n) for n in range(HEADS)] + [job for u in sorted(job_at) for job in job_at[u]]
        STEPS = max(job_at) + 1
        base = [0]
        for i, h in UNITS:
            base.append(base[-1] + len(transpose_steps(i)))

        half = HEADS * RANK // 2
        w_parts = [(wuk, wraw[0], io["w_uk"], slice(0, half)), (wuk, wraw[0], io["w_uk"], slice(half, 2 * half)),
                   (wuv, wraw[1], io["w_uv"], slice(0, 2 * half))]

        def queries(n, part):
            return q_first[part][:, n, :] if n < HEADS else q[part][:, n % HG, :]

        def queries_for(u):
            return [n // HG for kind, n in job_at.get(u, []) if kind == "absorb" and n % HG == 0]

        def order(job):
            return jobs.index(job)

        def splits_before(n):
            return sum(kind != "expand" for kind, _ in jobs[:n])

        def expands_before(n):
            return n - splits_before(n)

        def scores_at(u):
            pc = score_pieces(KEYS[UNITS[u][0]])
            first = 0 if len(pc) == 4 else 2 * (u % 2)
            return ps_s[:, first:first + len(pc), 0:pc[0][1]]

        def tile_columns(i):
            return slice(P * (i % GROUP), P * (i % GROUP) + P)

        def t_evicts(u):
            i, h = UNITS[u]
            for n, chunks in enumerate(transpose_steps(i)):
                m = base[u] + n
                full = [j for j in chunks if j > 0]
                pairs = []
                if full:
                    pairs.append((ps_t[:, m % 2, 0:len(full), :], slice(0, P), slice(full[0], full[-1] + 1)))
                if 0 in chunks:
                    pairs.append((ps_t[0:META, m % 2, len(full):len(full) + 1, :], slice(0, META), slice(0, 1)))
                yield m, pairs

        def bank(job):
            return ps_o[:, order(job) % 2, :]

        def result(job, part):
            kind, n = job
            if kind == "absorb":
                g, c = n // HEADS, RC * (n % HEADS)
                return lat[part][:, g % 2, c:c + RC, :], bank(job).rearrange("p (c n) -> p c n", n=GQ)
            i, h = UNITS[HG * n]
            return (lat[part][:, (i // GROUP) % 2, RC * h:RC * (h + HG), tile_columns(i)].rearrange(
                        "p (h r) n -> p r h n", r=RC),
                    bank(job).rearrange("p (r h n) -> p r h n", r=RC, h=HG))

        @block.sync
        def _(sp):
            def load_queries(m):
                g, h = m // PAIRS, HG * (m % PAIRS)
                if m > PAIRS:
                    sp.wait_ge(q_low, m)
                sp.dma_start(qraw[:, :, :], io["projT"][Q_T + h:Q_T + h + HG, :, META + GQ * g:META + GQ * (g + 1)
                                                        ].rearrange("h p n -> p h n")).then_inc(q_loaded, 16)

            def load_weights(n):
                w, raw, src, cols = w_parts[n]
                sp.dma_start(raw[:, cols], src[:, cols]).then_inc(w_loaded[n], 16)

            load_weights(0)
            sp.dma_start(f32(q_first[1]), io["projT"][Q_T:Q_T + HEADS, :, META:META + GQ].rearrange("h p n -> p h n")
                         ).then_inc(q_first_loaded, 16)
            load_weights(1)
            load_weights(2)
            load_queries(PAIRS)
            for u in range(STEPS):
                for m in queries_for(u):
                    if m + 1 < PAIRS * (NT // GROUP):
                        load_queries(m + 1)
                for kind, n in job_at.get(u, []):
                    if kind == "expand":
                        g, h = n // PAIRS, HG * (n % PAIRS)
                        sp.wait_ge(expanded, n + 1)
                        sp.dma_start(io["oT"][h:h + HG, :, GQ * g:GQ * (g + 1)].rearrange("h p n -> p h n"),
                                     out[:, n % 2, :, :]).then_inc(stored[n % 2], 16)
            for s in range(2):
                sp.wait_ge(stored[s], 16 * (PAIRS * (NT // GROUP) // 2))

        @block.gpsimd
        def _(pool):
            pool.memset(ident[:, :], 0.0).then_inc(id0, 1)
            pool.memset(maskb[:, 0:KEYS[0]], 0.0).then_inc(id0, 1)
            pool.wait_ge(id0, 2)
            pool.affine_select(out=ident[:, :], in_=ident[:, :], compare_op=ALU.not_equal, fill=1.0,
                               base=0, pattern=[[-1, P]], channel_multiplier=1).then_inc(id_ready, 1)
            for i in range(NT):
                at = MB_OFF[i] + KEYS[i] - P
                pool.affine_select(out=maskb[:, at:at + P], in_=maskb[:, at:at + P], compare_op=ALU.is_ge,
                                   fill=NEG, base=0, pattern=[[-1, P]], channel_multiplier=1).then_inc(causal, 1)

        @block.tensor
        def _(pe):
            def score(u):
                i, h = UNITS[u]
                if u % GU == 0:
                    pe.wait_ge(o_low, splits_before(order(("absorb", HEADS * (u // GU + 1) - 1)) + 1))
                if u >= 1 and (len(score_pieces(KEYS[i])) == 4):
                    pe.wait_ge(mask_added, u)
                elif u >= 2:
                    pe.wait_ge(mask_added, u - 1)
                for r in range(RC):
                    for n_pass, (a, b) in enumerate(PASSES):
                        for c, (at, w) in enumerate(score_pieces(KEYS[i])):
                            last = pe.matmul(scores_at(u)[:, c, :],
                                             lat[a][:, (u // GU) % 2, RC * h + r, tile_columns(i)],
                                             cT[b][:, r, at:at + w],
                                             start=(r == 0 and n_pass == 0), stop=(r == RC - 1 and n_pass == 2))
                last.then_inc(scored, 1)

            def turn(u):
                i, h = UNITS[u]
                pe.wait_ge(normed, u + 1)
                for n, chunks in enumerate(transpose_steps(i)):
                    m = base[u] + n
                    if m >= 2:
                        pe.wait_ge(t_low, m - 1)
                    for c, j in enumerate(chunks):
                        at, w = key_chunk(j)
                        last = pe.transpose(ps_t[0:w, m % 2, c, :], prob[:, u % 3, at:at + w], ident[:, :])
                    last.then_inc(turned, 1)

            def weigh(v, into):
                i, h = UNITS[HG * v]
                pe.wait_ge(t_low, base[HG * v + HG])
                for r in range(RC):
                    for n_pass, (a, b) in enumerate(PASSES):
                        for j in range(i + 2):
                            at, w = key_chunk(j)
                            last = pe.matmul(into[:, GQ * r:GQ * r + GQ], ctok[a][0:w, j, P * r:P * r + P],
                                             pT[b][0:w, v % 2, j, :, :].rearrange("p h n -> p (h n)"),
                                             start=(n_pass == 0 and j == 0), stop=(n_pass == 2 and j == i + 1))
                return last

            def absorb(n, into):
                if n >= HEADS:
                    pe.wait_ge(q_low, n // HG + 1)
                h = n % HEADS
                for r in range(RC):
                    for n_pass, (a, b) in enumerate(PASSES):
                        last = pe.matmul(into[:, GQ * r:GQ * r + GQ], wuk[a][:, RANK * h + P * r:RANK * h + P * r + P],
                                         queries(n, b), start=(n_pass == 0), stop=(n_pass == 2))
                return last

            def expand(n, into):
                g = n // PAIRS
                pe.wait_ge(o_low, splits_before(order(("weigh", GU // HG * (g + 1) - 1)) + 1))
                for e in range(HG):
                    h = HG * (n % PAIRS) + e
                    for r in range(RC):
                        for n_pass, (a, b) in enumerate(PASSES):
                            at = (r * HEADS + h) * P
                            last = pe.matmul(into[:, GQ * e:GQ * e + GQ], wuv[a][:, at:at + P],
                                             lat[b][:, g % 2, RC * h + r, :],
                                             start=(r == 0 and n_pass == 0), stop=(r == RC - 1 and n_pass == 2))
                return last

            def run(job):
                n = order(job)
                if n >= 2:
                    pe.wait_ge(o_low, splits_before(n - 1))
                    if expands_before(n - 1):
                        pe.wait_ge(expanded, expands_before(n - 1))
                kind = {"weigh": weigh, "absorb": absorb, "expand": expand}[job[0]]
                kind(job[1], bank(job)).then_inc(job_done, 1)

            pe.wait_ge(id_ready, 1)
            pe.wait_ge(q_low, PAIRS)
            for n in range(HEADS):
                pe.wait_ge(w_low, 1 + n // (HEADS // 2))
                run(("absorb", n))
            pe.wait_ge(w_low, 3)
            for u in range(STEPS):
                if u < U:
                    score(u)
                if 2 <= u < U + 2:
                    turn(u - 2)
                for job in job_at.get(u, []):
                    run(job)

        @block.scalar
        def _(act):
            def split_weights(n):
                w, raw, src, cols = w_parts[n]
                act.wait_ge(w_loaded[n], 16)
                act.activation(w[0][:, cols], raw[:, cols], ACT.Copy).then_inc(w_high, 1)

            def split_queries(m):
                act.wait_ge(q_loaded, 16 * (m - PAIRS + 1))
                if m > PAIRS:
                    act.wait_ge(job_done, order(("absorb", HG * m - 1)) + 1)
                act.activation(q[0][:, :, :], qraw[:, :, :], ACT.Copy).then_inc(q_high, 1)

            def finish(job):
                act.wait_ge(job_done, order(job) + 1)
                if job[0] == "expand":
                    n = job[1]
                    if n >= 2:
                        act.wait_ge(stored[n % 2], 16 * (n // 2))
                    act.activation(out[:, n % 2, :, :].rearrange("p e n -> p (e n)"), bank(job),
                                   ACT.Copy).then_inc(expanded, 1)
                else:
                    dst, src = result(job, 0)
                    act.activation(dst, src, ACT.Copy).then_inc(o_high, 1)

            def turn_high(u):
                i, h = UNITS[u]
                if u >= 2 * HG:
                    act.wait_ge(job_done, order(("weigh", u // HG - 2)) + 1)
                for m, pairs in t_evicts(u):
                    act.wait_ge(turned, m + 1)
                    for src, rows, js in pairs:
                        last = act.activation(pT[0][rows, (u // HG) % 2, js, u % HG, :], src, ACT.Copy)
                    last.then_inc(t_high, 1)

            split_weights(0)
            act.wait_ge(q_first_loaded, 16)
            act.activation(q_first[0], f32(q_first[1]), ACT.Copy).then_inc(q_high, PAIRS)
            split_weights(1)
            for n in range(HEADS):
                finish(("absorb", n))
                if n == 0:
                    split_weights(2)
            act.wait_ge(w_low, 3)
            for u in range(STEPS):
                if 2 <= u < U + 2:
                    turn_high(u - 2)
                for job in job_at.get(u, []):
                    finish(job)
                if u < U:
                    act.wait_ge(biased, u + 1)
                    if u >= 3:
                        act.wait_ge(turned, base[u - 2])
                    n = KEYS[UNITS[u][0]]
                    act.activation(prob[:, u % 3, 0:n], masked[:, u % 2, 0:n], ACT.Exp, bias=bias[:, u:u + 1],
                                   scale=SCALE, accum_out=total[:, u:u + 1]).then_inc(exped, 1)
                for m in queries_for(u + 1):
                    split_queries(m)

        @block.vector
        def _(dve):
            def split_weights(n):
                w, raw, src, cols = w_parts[n]
                dve.wait_ge(w_high, n + 1)
                dve.tensor_tensor(w[1][:, cols], raw[:, cols], f32(w[0][:, cols]), ALU.subtract).then_inc(w_low, 1)

            def split_queries(m):
                dve.wait_ge(q_high, m + 1)
                dve.tensor_tensor(q[1][:, :, :], qraw[:, :, :], f32(q[0][:, :, :]), ALU.subtract).then_inc(q_low, 1)

            def finish(job):
                if job[0] != "expand":
                    dve.wait_ge(o_high, splits_before(order(job)) + 1)
                    dst, src = result(job, 1)
                    dve.tensor_tensor(dst, src, f32(result(job, 0)[0]), ALU.subtract).then_inc(o_low, 1)

            def turn_low(u):
                for m, pairs in t_evicts(u):
                    dve.wait_ge(t_high, m + 1)
                    for src, rows, js in pairs:
                        high, low = (m[rows, (u // HG) % 2, js, u % HG, :] for m in pT)
                        last = dve.tensor_tensor(low, src, f32(high), ALU.subtract)
                    last.then_inc(t_low, 1)

            def add_mask(u):
                i, h = UNITS[u]
                n = KEYS[i]
                pc = score_pieces(n)
                if h == 0:
                    dve.wait_ge(causal, i + 1)
                dve.wait_ge(scored, u + 1)
                if u >= 2:
                    dve.wait_ge(exped, u - 1)
                dve.tensor_tensor_reduce(
                    masked[:, u % 2, 0:n].rearrange("p (c n) -> p c n", c=len(pc)), scores_at(u),
                    maskb[:, MB_OFF[i]:MB_OFF[i] + n].rearrange("p (c n) -> p c n", c=len(pc)),
                    1.0, 3 * NEG, ALU.add, ALU.max, top[:, u:u + 1]).then_inc(mask_added, 1)
                dve.drain()
                dve.tensor_scalar(bias[:, u:u + 1], top[:, u:u + 1], -SCALE, None, ALU.mult).then_inc(biased, 1)

            def normalise(u):
                n = KEYS[UNITS[u][0]]
                dve.wait_ge(exped, u + 1)
                dve.reciprocal(inv[:, u:u + 1], total[:, u:u + 1])
                dve.drain()
                dve.tensor_scalar(prob[:, u % 3, 0:n], prob[:, u % 3, 0:n], inv[:, u:u + 1], None,
                                  ALU.mult).then_inc(normed, 1)

            split_weights(0)
            dve.wait_ge(q_high, PAIRS)
            dve.tensor_tensor(q_first[1], f32(q_first[1]), f32(q_first[0]), ALU.subtract).then_inc(q_low, PAIRS)
            split_weights(1)
            for n in range(HEADS):
                finish(("absorb", n))
                if n == 0:
                    split_weights(2)
            dve.drain()
            for u in range(STEPS):
                if u < U:
                    add_mask(u)
                if 1 <= u < U + 1:
                    normalise(u - 1)
                if 2 <= u < U + 2:
                    turn_low(u - 2)
                for job in job_at.get(u, []):
                    finish(job)
                for m in queries_for(u + 1):
                    split_queries(m)


PARAMS = ("conv0", "conv1", "conv2", "conv3", "conv_b", "b_a", "b_x", "lam")
PAD = 3


def stage_recurrent(nc, io):
    with Kit(nc, "lru") as k:
        par = k.sb("par", [P, len(PARAMS), NB])
        rate = k.sb("rate", [P, NB])
        tmp = k.sb("tmp", [P, 6, NB])
        unit = k.sb("unit", [P, NB], I32)
        x = k.sb("x", [P, 2, PAD + T])
        gelu = k.sb("gelu", [P, 2, S])
        conv = k.sb("conv", [P, 2, T])
        xs = [k.sb("x_high", [P, 2, T], F32R), k.sb("x_low", [P, 2, T], F32R)]
        wraw = k.sb("wraw", [P, 2, 2 * P])
        w = [k.sb("w_high", [P, 2, 2 * P], F32R), k.sb("w_low", [P, 2, 2 * P], F32R)]
        r = k.sb("r", [P, T])
        gate = k.sb("gate", [P, T])
        a = k.sb("a", [P, 2, T])
        th = k.sb("th", [P, T])
        square = k.sb("square", [P, T])
        root = k.sb("root", [P, T])
        gated = k.sb("gated", [P, T])
        hid = k.sb("hid", [P, T])
        out = k.sb("out", [P, 2, S])
        ps = k.ps("ps", [P, 2, 3, 512])
        loaded_p, exponent_ready, exp_ready, one_plus_ready, log_ready, rate_ready = (k.sem(n) for n in (
            "loaded_p", "exponent_ready", "exp_ready", "one_plus_ready", "log_ready", "rate_ready"))
        loaded = [k.sem("loaded0"), k.sem("loaded1")]
        gelu_loaded = [k.sem("gelu_loaded0"), k.sem("gelu_loaded1")]
        stored = [k.sem("stored0"), k.sem("stored1")]
        (conv_done, high, low, done_r, r_ready, done_x, gate_ready, acted, folded, root_ready, x_gated,
         input_ready, scanned, outed) = (k.sem(n) for n in (
             "conv_done", "high", "low", "done_r", "r_ready", "done_x", "gate_ready", "acted", "folded",
             "root_ready", "x_gated", "input_ready", "scanned", "outed"))
        oraw = k.sb("oraw", [P, 4, S])
        os_ = [k.sb("o_high", [P, HEADS, S], F32R), k.sb("o_low", [P, HEADS, S], F32R)]
        braw = k.sb("braw", [P, HEADS, P])
        bw = [k.sb("bw_high", [P, 2, HEADS, P], F32R), k.sb("bw_low", [P, 2, HEADS, P], F32R)]
        bgate = k.sb("bgate", [P, 2, S])
        psb = k.ps("psb", [P, 2, 512])
        o_loaded = [k.sem(f"o_loaded{c}") for c in range(4)]
        bw_loaded = k.sem("bw_loaded")
        bg_loaded = [k.sem("bg_loaded0"), k.sem("bg_loaded1")]
        b_stored = [k.sem("b_stored0"), k.sem("b_stored1")]
        o_high, o_low, bw_high, bw_low, b_done, b_ready = (k.sem(n) for n in (
            "o_high_ready", "o_low_ready", "bw_high_ready", "bw_low_ready", "b_done", "b_ready"))
        block = k.block()

        def p(name, b):
            return par[:, PARAMS.index(name), bass.ds(b, 1)]

        def loop(eng, step):
            for n in range(4):
                step(n, n % 2, n // 2)
            with eng.Fori(2, NB // 2 - 1) as j:
                step(2 * j, 0, j)
                step(2 * j + 1, 1, j)
            for n in range(NB - 2, NB):
                step(n, n % 2, n // 2)

        def before(n, k):
            return type(n) is int and n < k

        def is_last(n):
            return type(n) is int and n == NB - 1

        def before_last(n, k):
            return type(n) is int and n >= NB - 1 - k

        @block.sync
        def _(sp):
            sp.dma_start(par[:, :, :], io["lru_params"]).then_inc(loaded_p, 16)

            def load(b, s):
                if not before(b, 2):
                    sp.wait_ge(low, b - 1)
                sp.dma_start(x[:, s, PAD:PAD + T], io["projT"][bass.ds(b + X_LRU, 1)].rearrange("a p n -> (a p) n")
                             ).then_inc(loaded[s], 16)
                sp.dma_start(wraw[:, s, :], io["w_rg"][bass.ds(b, 1)].rearrange("a p n -> (a p) n")
                             ).then_inc(loaded[s], 16)

            def load_gelu(b, s):
                if not before(b, 2):
                    sp.wait_ge(outed, b - 1)
                sp.dma_start(gelu[:, s, :], io["projT"][bass.ds(b + G_LRU, 1), :, META:T].rearrange(
                    "a p n -> (a p) n")).then_inc(gelu_loaded[s], 16)

            def load_tile_weights(m):
                if not before(m, 1):
                    sp.wait_ge(bw_low, m)
                sp.dma_start(braw[:, :, :], io["w_branch_b"][bass.ds(m, 1)].rearrange("a p c n -> p (a c) n")
                             ).then_inc(bw_loaded, 16)

            load(0, 0)
            load(1, 1)
            load_gelu(0, 0)

            def load_heads(half):
                for c in range(HEADS // 2 * half, HEADS // 2 * (half + 1)):
                    if c >= 4:
                        sp.wait_ge(o_low, c - 3)
                    sp.dma_start(oraw[:, c % 4, :], io["oT"][c]).then_inc(o_loaded[c % 4], 16)

            def store_block(n, s):
                sp.wait_ge(outed, n + 1)
                sp.dma_start(io["yaT"][bass.ds(n, 1)].rearrange("a p n -> (a p) n"), out[:, s, :]
                               ).then_inc(stored[s], 16)

            def store_tile(m, s):
                sp.wait_ge(b_ready, m + 1)
                sp.dma_start(io["ybT"][bass.ds(m, 1)].rearrange("a p n -> (a p) n"), bgate[:, s, :]
                               ).then_inc(b_stored[s], 16)

            def step(n, s, i):
                if not before_last(n, 1):
                    load(n + 2, s)
                if not is_last(n):
                    load_gelu(n + 1, 1 - s)
                if not before(n, 1):
                    store_block(n - 1, 1 - s)
                if not (before(n, 1) or is_last(n)):
                    load_tile_weights(n - 1)
                if not before(n, 2):
                    if not before(n, 4):
                        sp.wait_ge(b_stored[s], 16 * i - 16)
                    sp.dma_start(bgate[:, s, :], io["projT"][bass.ds(n + (GATE_B - 2), 1), :, META:T].rearrange(
                        "a p n -> (a p) n")).then_inc(bg_loaded[s], 16)
                if before(n, 2):
                    load_heads(n)
                if not before(n, 3):
                    store_tile(n - 3, 1 - s)
            loop(sp, step)
            store_tile(KC - 1, 1)
            store_block(NB - 1, 1)
            for s in range(2):
                sp.wait_ge(stored[s], 16 * (NB // 2))
                sp.wait_ge(b_stored[s], 16 * (KC // 2))

        @block.gpsimd
        def _(pool):
            def step(n, s, i):
                pool.wait_ge(gate_ready, n + 1)
                if not before(n, 1):
                    pool.wait_ge(input_ready, n)
                pool.tensor_tensor(gated[:, :], gate[:, :], conv[:, s, :], ALU.mult).then_inc(x_gated, 1)
            loop(pool, step)

        @block.tensor
        def _(pe):
            def gates(b, s, m, done):
                for n_pass, (wa, xb) in enumerate(PASSES):
                    for q, (at, n) in enumerate(TOK3):
                        last = pe.matmul(ps[:, m, q, 0:n], w[wa][:, s, P * m:P * m + P], xs[xb][:, s, at:at + n],
                                         start=(n_pass == 0), stop=(n_pass == 2))
                last.then_inc(done, 1)

            def branch(m, s, head_waits):
                for c in range(HEADS):
                    if head_waits:
                        pe.wait_ge(o_low, c + 1)
                    for n_pass, (wa, xb) in enumerate(PASSES):
                        for q in range(2):
                            last = pe.matmul(psb[:, q, :], bw[wa][:, s, c, :], os_[xb][:, c, 512 * q:512 * q + 512],
                                             start=(c == 0 and n_pass == 0), stop=(c == HEADS - 1 and n_pass == 2))
                last.then_inc(b_done, 1)

            def step(n, s, i):
                pe.wait_ge(low, n + 1)
                if not before(n, 1):
                    pe.wait_ge(r_ready, n)
                gates(n, s, 0, done_r)
                if not before(n, 1):
                    pe.wait_ge(gate_ready, n)
                gates(n, s, 1, done_x)
                if not before(n, 2):
                    pe.wait_ge(bw_low, n - 1)
                    if not before(n, 3):
                        pe.wait_ge(b_ready, n - 2)
                    branch(n - 2, s, before(n, 3))
            loop(pe, step)

        @block.scalar
        def _(act):
            def prepare(b, s):
                act.wait_ge(conv_done, b + 1)
                if not before(b, 2):
                    act.wait_ge(done_x, b - 1)
                act.activation(xs[0][:, s, :], conv[:, s, :], ACT.Copy)
                act.activation(w[0][:, s, :], wraw[:, s, :], ACT.Copy).then_inc(high, 1)

            prepare(0, 0)
            act.wait_ge(exponent_ready, 1)
            act.activation(tmp[:, 1, :], tmp[:, 0, :], ACT.Exp).then_inc(exp_ready, 1)
            act.wait_ge(one_plus_ready, 1)
            act.activation(tmp[:, 3, :], tmp[:, 2, :], ACT.Ln).then_inc(log_ready, 1)

            def sigmoid(dst, m, b):
                at, width = TOK3[2]
                act.activation(dst[:, 0:at].rearrange("p (c n) -> p c n", c=2), ps[:, m, 0:2, 0:at // 2],
                               ACT.Sigmoid, bias=b)
                return act.activation(dst[:, at:at + width], ps[:, m, 2, 0:width], ACT.Sigmoid, bias=b)

            def step(n, s, i):
                act.drain()
                act.wait_ge(done_r, n + 1)
                sigmoid(r, 0, p("b_a", n)).then_inc(r_ready, 1)
                act.wait_ge(done_x, n + 1)
                if not before(n, 1):
                    act.wait_ge(x_gated, n)
                sigmoid(gate, 1, p("b_x", n)).then_inc(gate_ready, 1)
                act.drain()
                if not before(n, 2):
                    act.wait_ge(scanned, n - 1)
                if before(n, 1):
                    act.wait_ge(rate_ready, 1)
                act.activation(a[:, s, :], r[:, :], ACT.Exp, scale=rate[:, bass.ds(n, 1)])
                act.activation(th[:, :], r[:, :], ACT.Tanh, scale=rate[:, bass.ds(n, 1)])
                act.drain()
                act.activation(square[:, :], a[:, s, :], ACT.Square).then_inc(acted, 1)
                if not is_last(n):
                    prepare(n + 1, 1 - s)
                if not (before(n, 1) or is_last(n)):
                    act.wait_ge(bw_loaded, 16 * n)
                    if not before(n, 3):
                        act.wait_ge(b_done, n - 2)
                    act.activation(bw[0][:, 1 - s], braw[:, :, :], ACT.Copy).then_inc(bw_high, 1)
                act.wait_ge(folded, n + 1)
                if not before(n, 1):
                    act.wait_ge(scanned, n)
                act.activation(root[:, :], th[:, :], ACT.Sqrt, scale=-1.0).then_inc(root_ready, 1)
                if before(n, 2):
                    for c in range(HEADS // 2 * n, HEADS // 2 * (n + 1)):
                        act.wait_ge(o_loaded[c % 4], 16 * (c // 4 + 1))
                        act.activation(os_[0][:, c, :], oraw[:, c % 4, :], ACT.Copy).then_inc(o_high, 1)
            loop(act, step)

        @block.vector
        def _(dve):
            lam = par[:, PARAMS.index("lam"), :]
            for s in range(2):
                dve.memset(x[:, s, 0:PAD], 0.0)
            dve.drain()
            dve.wait_ge(loaded_p, 16)

            def prepare(b, s, trips):
                dve.wait_ge(loaded[s], 32 * trips)
                if not before(b, 2):
                    dve.wait_ge(x_gated, b - 1)
                dve.tensor_scalar(conv[:, s, :], x[:, s, 0:T], p("conv0", b), p("conv_b", b), ALU.mult, ALU.add)
                for t in range(1, 4):
                    dve.drain()
                    last = dve.scalar_tensor_tensor(out=conv[:, s, :], in0=x[:, s, t:t + T], scalar=p(f"conv{t}", b),
                                                    in1=conv[:, s, :], op0=ALU.mult, op1=ALU.add)
                last.then_inc(conv_done, 1)

            def split_low(b, s):
                dve.wait_ge(high, b + 1)
                dve.tensor_tensor(xs[1][:, s, :], conv[:, s, :], f32(xs[0][:, s, :]), ALU.subtract)
                dve.tensor_tensor(w[1][:, s, :], wraw[:, s, :], f32(w[0][:, s, :]), ALU.subtract).then_inc(low, 1)

            prepare(0, 0, 1)
            split_low(0, 0)
            dve.tensor_scalar(tmp[:, 5, :], lam, -1.0, None, ALU.mult)
            dve.drain()
            dve.tensor_tensor(tmp[:, 0, :], tmp[:, 5, :], lam, ALU.min).then_inc(exponent_ready, 1)
            dve.wait_ge(exp_ready, 1)
            dve.tensor_scalar(tmp[:, 2, :], tmp[:, 1, :], 1.0, None, ALU.add).then_inc(one_plus_ready, 1)
            dve.wait_ge(log_ready, 1)
            dve.tensor_scalar(tmp[:, 4, :], tmp[:, 2, :], -1.0, 1e-30, ALU.add, ALU.max)
            dve.tensor_scalar(unit[:, :], tmp[:, 2, :], 1.0, None, ALU.is_equal)
            dve.drain()
            dve.reciprocal(tmp[:, 2, :], tmp[:, 4, :])
            dve.drain()
            dve.tensor_tensor(tmp[:, 2, :], tmp[:, 2, :], tmp[:, 1, :], ALU.mult)
            dve.drain()
            dve.tensor_tensor(tmp[:, 3, :], tmp[:, 3, :], tmp[:, 2, :], ALU.mult)
            dve.drain()
            dve.copy_predicated(tmp[:, 3, :], unit[:, :], tmp[:, 1, :])
            dve.drain()
            dve.scalar_tensor_tensor(out=tmp[:, 3, :], in0=tmp[:, 5, :], scalar=0.0, in1=tmp[:, 3, :],
                                     op0=ALU.max, op1=ALU.add)
            dve.drain()
            dve.tensor_scalar(rate[:, :], tmp[:, 3, :], -8.0, None, ALU.mult).then_inc(rate_ready, 1)
            dve.drain()


            def gate_tile(m, s, trips):
                dve.wait_ge(bg_loaded[s], 16 * trips)
                dve.wait_ge(b_done, m + 1)
                g2 = bgate[:, s, :].rearrange("p (b n) -> p b n", b=2)
                dve.tensor_tensor(g2, psb[:, :, :], g2, ALU.mult).then_inc(b_ready, 1)

            def step(n, s, i):
                if not before(n, 3):
                    gate_tile(n - 3, 1 - s, i - 1 + s)
                if not is_last(n):
                    prepare(n + 1, 1 - s, i + 1 + s)
                dve.wait_ge(acted, n + 1)
                dve.scalar_tensor_tensor(out=th[:, :], in0=square[:, :], scalar=1.0, in1=th[:, :], op0=ALU.add,
                                         op1=ALU.mult).then_inc(folded, 1)
                if not is_last(n):
                    split_low(n + 1, 1 - s)
                if not (before(n, 1) or is_last(n)):
                    dve.wait_ge(bw_high, n)
                    dve.tensor_tensor(bw[1][:, 1 - s], braw[:, :, :], f32(bw[0][:, 1 - s]), ALU.subtract
                                      ).then_inc(bw_low, 1)
                dve.wait_ge(x_gated, n + 1)
                dve.wait_ge(root_ready, n + 1)
                dve.tensor_tensor(root[:, :], root[:, :], gated[:, :], ALU.mult).then_inc(input_ready, 1)
                dve.wait_ge(input_ready, n + 1)
                dve.tensor_tensor_scan(hid[:, :], a[:, s, :], root[:, :], 0.0, ALU.mult, ALU.add).then_inc(scanned, 1)
                if not before(n, 2):
                    dve.wait_ge(stored[s], 16 * i)
                dve.wait_ge(scanned, n + 1)
                dve.wait_ge(gelu_loaded[s], 16 * i + 16)
                dve.tensor_tensor(out[:, s, :], hid[:, META:T], gelu[:, s, :], ALU.mult).then_inc(outed, 1)
                if before(n, 2):
                    for c in range(HEADS // 2 * n, HEADS // 2 * (n + 1)):
                        dve.wait_ge(o_high, c + 1)
                        dve.tensor_tensor(os_[1][:, c, :], oraw[:, c % 4, :], f32(os_[0][:, c, :]),
                                          ALU.subtract).then_inc(o_low, 1)
            loop(dve, step)
            gate_tile(KC - 1, 1, KC // 2)


def stage_branch(nc, io, mixed):
    with Kit(nc, "bra") as k:
        xraw = k.sb("xraw", [P, 4, S])
        xs = [k.sb("x_high", [P, NB, S], F32R), k.sb("x_low", [P, NB, S], F32R)]
        wraw = k.sb("wraw", [P, NB, P])
        w = [k.sb("w_high", [P, 2, NB, P], F32R), k.sb("w_low", [P, 2, NB, P], F32R)]
        gin = k.sb("gin", [P, 2, S])
        other = k.sb("other", [P, S])
        ps = k.ps("ps", [P, 2, 2, 512])
        x_loaded = [k.sem(f"x_loaded{c}") for c in range(4)]
        w_loaded, g_loaded, o_loaded = k.sem("w_loaded"), [k.sem("g_loaded0"), k.sem("g_loaded1")], k.sem("o_loaded")
        x_high, x_low, w_high, w_low, done, ready, high, low = (
            k.sem(n) for n in ("x_high_ready", "x_low_ready", "w_high_ready", "w_low_ready", "done",
                               "ready", "high", "low"))
        block = k.block()

        @block.sync
        def _(sp):
            for c in range(NB):
                if c >= 4:
                    sp.wait_ge(x_low, c - 3)
                sp.dma_start(xraw[:, c % 4, :], io["yaT"][c]).then_inc(x_loaded[c % 4], 16)
                if c == 1:
                    sp.dma_start(wraw[:, :, :], io["w_branch_a"][0]).then_inc(w_loaded, 16)
            for m in range(KC):
                if m >= 1:
                    sp.wait_ge(w_low, m)
                    sp.dma_start(wraw[:, :, :], io["w_branch_a"][m]).then_inc(w_loaded, 16)
                if m >= 2:
                    sp.wait_ge(ready, m - 1)
                sp.dma_start(gin[:, m % 2, :], io["projT"][GATE_A + m, :, META:T]).then_inc(g_loaded[m % 2], 16)
                if m >= 1:
                    sp.wait_ge(o_loaded, 16 * m)
                    sp.wait_ge(low, m)
                sp.dma_start(other[:, :], io["ybT"][m]).then_inc(o_loaded, 16)

        @block.scalar
        def _(act):
            def w_split(m):
                act.wait_ge(w_loaded, 16 * (m + 1))
                if m >= 2:
                    act.wait_ge(done, m - 1)
                act.activation(w[0][:, m % 2], wraw[:, :, :], ACT.Copy).then_inc(w_high, 1)

            for c in range(NB):
                act.wait_ge(x_loaded[c % 4], 16 * (c // 4 + 1))
                act.activation(xs[0][:, c, :], xraw[:, c % 4, :], ACT.Copy).then_inc(x_high, 1)
                if c == 1:
                    w_split(0)
            for m in range(KC):
                if m + 1 < KC:
                    w_split(m + 1)
                act.wait_ge(ready, m + 1)
                act.activation(mixed[0][:, m, :], other[:, :], ACT.Copy).then_inc(high, 1)

        @block.vector
        def _(dve):
            def w_split(m):
                dve.wait_ge(w_high, m + 1)
                dve.tensor_tensor(w[1][:, m % 2], wraw[:, :, :], f32(w[0][:, m % 2]), ALU.subtract).then_inc(w_low, 1)

            for c in range(NB):
                dve.wait_ge(x_high, c + 1)
                dve.tensor_tensor(xs[1][:, c, :], xraw[:, c % 4, :], f32(xs[0][:, c, :]),
                                  ALU.subtract).then_inc(x_low, 1)
                if c == 1:
                    w_split(0)
            for m in range(KC):
                if m + 1 < KC:
                    w_split(m + 1)
                dve.wait_ge(g_loaded[m % 2], 16 * (m // 2 + 1))
                dve.wait_ge(done, m + 1)
                g2 = gin[:, m % 2, :].rearrange("p (b n) -> p b n", b=2)
                dve.tensor_tensor(g2, ps[:, m % 2], g2, ALU.mult)
                dve.drain()
                dve.wait_ge(o_loaded, 16 * (m + 1))
                dve.tensor_tensor(other[:, :], other[:, :], gin[:, m % 2, :], ALU.add).then_inc(ready, 1)
                dve.wait_ge(high, m + 1)
                dve.tensor_tensor(mixed[1][:, m, :], other[:, :], f32(mixed[0][:, m, :]),
                                  ALU.subtract).then_inc(low, 1)
            dve.wait_ge(low, KC)

        @block.tensor
        def _(pe):
            for m in range(KC):
                pe.wait_ge(w_low, m + 1)
                if m >= 2:
                    pe.wait_ge(ready, m - 1)
                for c in range(NB):
                    if m == 0:
                        pe.wait_ge(x_low, c + 1)
                    for n_pass, (a, b) in enumerate(PASSES):
                        for q in range(2):
                            last = pe.matmul(ps[:, m % 2, q, :], w[a][:, m % 2, c, :],
                                             xs[b][:, c, 512 * q:512 * q + 512],
                                             start=(c == 0 and n_pass == 0), stop=(c == NB - 1 and n_pass == 2))
                last.then_inc(done, 1)


def stage_out(nc, io, mixed, acc):
    with Kit(nc, "out") as k:
        raw = k.sb("raw", [P, 4, D])
        w = [k.sb("w_high", [P, KC, D], F32R), k.sb("w_low", [P, KC, D], F32R)]
        hin = k.sb("hin", [P, 2, D])
        x1 = k.sb("x1", [P, 2, D])
        gain, shift, bd = (k.sb(n, [P, D]) for n in ("gain", "shift", "bd"))
        ident = k.sb("ident", [P, P])
        stats = k.sb("stats", [P, 2, 6])
        mv = k.sb("mv", [P, 2])
        eps, var, sd, rs, tmp = (k.sb(n, [P, 1]) for n in ("eps", "var", "sd", "rs", "tmp"))
        ps = k.ps("ps", [P, 2, 2, 512])
        psT = k.ps("psT", [P, 2, 2, 512])
        w_loaded = [k.sem(f"w_loaded{c}") for c in range(4)]
        h_loaded = [k.sem("h_loaded0"), k.sem("h_loaded1")]
        (consts, id0, id_ready, w_high, w_low, done, residual, var_ready, sd_ready, x1_ready, transposed, high,
         low) = (k.sem(n) for n in (
             "consts", "id0", "id_ready", "w_high_ready", "w_low_ready", "done", "residual", "var_ready", "sd_ready",
             "x1_ready", "transposed", "high", "low"))
        block = k.block()

        def psum_of(t):
            return psT[:, t % 2].rearrange("p b (c n) -> p (b c) n", c=4)

        def columns(t):
            return slice(P * t, P * t + P)

        @block.sync
        def _(sp):
            for c in range(KC):
                if c >= 4:
                    sp.wait_ge(w_low, c - 3)
                sp.dma_start(raw[:, c % 4, :], io["w_out"][P * c:P * c + P, :]).then_inc(w_loaded[c % 4], 16)
            for dst, name in ((gain, "ln1_g"), (shift, "ln1_b"), (bd, "b_down")):
                sp.dma_start(dst[:, :], io[name].partition_broadcast(P)).then_inc(consts, 16)
            for t in range(NT):
                if t >= 2:
                    sp.wait_ge(x1_ready, t - 1)
                sp.dma_start(hin[:, t % 2, :], io["h_tok"][t]).then_inc(h_loaded[t % 2], 16)

        @block.gpsimd
        def _(pool):
            pool.memset(ident[:, :], 0.0).then_inc(id0, 1)
            pool.wait_ge(id0, 1)
            pool.affine_select(out=ident[:, :], in_=ident[:, :], compare_op=ALU.not_equal, fill=1.0,
                               base=0, pattern=[[-1, P]], channel_multiplier=1).then_inc(id_ready, 1)

        @block.scalar
        def _(act):
            def split_high(t):
                act.wait_ge(transposed, t + 1)
                act.activation(mixed[0][:, :, columns(t)], psum_of(t), ACT.Copy).then_inc(high, 1)

            for c in range(KC):
                act.wait_ge(w_loaded[c % 4], 16 * (c // 4 + 1))
                act.activation(w[0][:, c, :], raw[:, c % 4, :], ACT.Copy).then_inc(w_high, 1)
            for t in range(NT):
                act.wait_ge(var_ready, t + 1)
                act.activation(sd[:, :], var[:, :], ACT.Sqrt).then_inc(sd_ready, 1)
                if t >= 1:
                    split_high(t - 1)
            split_high(NT - 1)

        @block.vector
        def _(dve):
            def split_low(t):
                dve.wait_ge(high, t + 1)
                dve.tensor_tensor(mixed[1][:, :, columns(t)], psum_of(t), f32(mixed[0][:, :, columns(t)]),
                                  ALU.subtract).then_inc(low, 1)

            dve.memset(eps[:, :], EPS)
            for c in range(KC):
                dve.wait_ge(w_high, c + 1)
                dve.tensor_tensor(w[1][:, c, :], raw[:, c % 4, :], f32(w[0][:, c, :]), ALU.subtract).then_inc(w_low, 1)
            for t in range(NT):
                r = hin[:, t % 2, :]
                dve.wait_ge(h_loaded[t % 2], 16 * (t // 2 + 1))
                dve.wait_ge(done, t + 1)
                r2 = r.rearrange("p (b n) -> p b n", b=2)
                dve.scalar_tensor_tensor(out=r2, in0=r2, scalar=ALPHA, in1=ps[:, t % 2], op0=ALU.mult,
                                         op1=ALU.add).then_inc(residual, 1)
                dve.drain()
                for c in range(2):
                    dve.bn_stats(stats[:, c, :], r[:, 512 * c:512 * c + 512])
                dve.drain()
                dve.bn_aggr(mv[:, :], stats[:, :, :])
                dve.drain()
                dve.tensor_tensor(var[:, :], mv[:, 1:2], eps[:, :], ALU.add).then_inc(var_ready, 1)
                dve.wait_ge(sd_ready, t + 1)
                refine_rsqrt(dve, var[:, :], sd[:, :], rs[:, :], tmp[:, :])
                dve.tensor_scalar(r, r, mv[:, 0:1], rs[:, 0:1], ALU.subtract, ALU.mult)
                dve.drain()
                if t == 0:
                    dve.wait_ge(consts, 48)
                if t >= 2:
                    dve.wait_ge(transposed, t - 1)
                dve.tensor_tensor(x1[:, t % 2, :], r, gain[:, :], ALU.mult)
                dve.drain()
                dve.tensor_tensor(x1[:, t % 2, :], x1[:, t % 2, :], shift[:, :], ALU.add).then_inc(x1_ready, 1)
                dve.drain()
                dve.scalar_tensor_tensor(out=acc[:, t, :], in0=x1[:, t % 2, :], scalar=ALPHA, in1=bd[:, :],
                                         op0=ALU.mult, op1=ALU.add)
                if t >= 1:
                    split_low(t - 1)
            split_low(NT - 1)

        @block.tensor
        def _(pe):
            def transpose(t):
                pe.wait_ge(x1_ready, t + 1)
                if t >= 2:
                    pe.wait_ge(low, t - 1)
                for c in range(KC):
                    last = pe.transpose(psum_of(t)[:, c, :], x1[:, t % 2, P * c:P * c + P], ident[:, :])
                last.then_inc(transposed, 1)

            for t in range(NT):
                if t >= 2:
                    pe.wait_ge(residual, t - 1)
                for c in range(KC):
                    if t == 0:
                        pe.wait_ge(w_low, c + 1)
                    for n_pass, (a, b) in enumerate(PASSES):
                        for q in range(2):
                            last = pe.matmul(ps[:, t % 2, q, :], mixed[a][:, c, columns(t)],
                                             w[b][:, c, 512 * q:512 * q + 512],
                                             start=(c == 0 and n_pass == 0), stop=(c == KC - 1 and n_pass == 2))
                last.then_inc(done, 1)
                if t == 0:
                    pe.wait_ge(id_ready, 1)
                else:
                    transpose(t - 1)
            transpose(NT - 1)


FG = 2
NG = NF // FG


def stage_mlp(nc, io, xT, acc):
    with Kit(nc, "mlp") as k:
        bu = k.sb("bu", [P, NF])
        uraw = k.sb("uraw", [P, FG, KC, P])
        ups = [k.sb("up_high", [P, FG, KC, P], F32R), k.sb("up_low", [P, FG, KC, P], F32R)]
        hid = k.sb("hid", [P, FG, S])
        hs = [k.sb("hs_high", [P, 2, FG, S], F32R), k.sb("hs_low", [P, 2, FG, S], F32R)]
        draw = k.sb("draw", [P, FG, D])
        dn = [k.sb("dn_high", [P, 2, FG, D], F32R), k.sb("dn_low", [P, 2, FG, D], F32R)]
        gain, shift = hid[:, 0, :], hid[:, 1, :]
        stats = k.sb("stats", [P, NT, 2, 6])
        mv = k.sb("mv", [P, NT, 2])
        eps = k.sb("eps", [P, 1])
        var, sd, scale, bias, tmp = (k.sb(n, [P, NT]) for n in ("var", "sd", "scale", "bias", "tmp"))
        ps_u = k.ps("ps_u", [P, FG, 2, 512])
        ps_d = k.ps("ps_d", [P, 2, 2, 512])
        bu_loaded, ln_loaded = k.sem("bu_loaded"), k.sem("ln_loaded")
        u_loaded = [k.sem("u_loaded0"), k.sem("u_loaded1")]
        d_loaded = [k.sem("d_loaded0"), k.sem("d_loaded1")]
        (u_high, u_low, up_done, rectified, squared, s_high, s_low, d_high, d_low, dn_done, added) = (
            k.sem(n) for n in ("u_high", "u_low", "up_done", "rectified", "squared", "s_high", "s_low", "d_high",
                               "d_low", "dn_done", "added"))
        var_ready, sd_ready, scale_ready, normalised, gained, stored = (k.sem(n) for n in (
            "var_ready", "sd_ready", "scale_ready", "normalised", "gained", "stored"))
        ready = [k.sem("ready_even"), k.sem("ready_odd")]
        block = k.block()

        def loop(eng, turn):
            turn(0, 0)
            turn(1, 1)
            with eng.Fori(1, NG // 2 - 1) as j:
                turn(2 * j, 0)
                turn(2 * j + 1, 1)
            turn(NG - 2, 0)
            turn(NG - 1, 1)

        def before(g, n):
            return type(g) is int and g < n

        def has_next(g, n):
            return not (type(g) is int and g + n >= NG)

        @block.sync
        def _(sp):
            def load_up(g, f):
                if not before(g, 1):
                    sp.wait_ge(u_low, FG * g + (f - 1))
                sp.dma_start(uraw[:, f, :, :], io["w_up"][bass.ds(FG * g + f, 1)].rearrange("a p c n -> p (a c) n")
                             ).then_inc(u_loaded[f], 16)

            def load_down(g, f):
                if not before(g, 1):
                    sp.wait_ge(d_low, FG * g + (f - 1))
                sp.dma_start(draw[:, f, :], io["w_down"][bass.ds(FG * g + f, 1)].rearrange("a p n -> p (a n)")
                             ).then_inc(d_loaded[f], 16)

            load_up(0, 0)
            load_up(0, 1)
            sp.dma_start(bu[:, :], io["b_up"]).then_inc(bu_loaded, 16)
            load_up(1, 0)
            load_up(1, 1)
            load_down(0, 0)
            load_down(0, 1)

            def turn(g, s):
                if has_next(g, 1):
                    load_down(g + 1, 0)
                    load_down(g + 1, 1)
                if has_next(g, 2):
                    load_up(g + 2, 0)
                    load_up(g + 2, 1)
            loop(sp, turn)
            sp.wait_ge(s_low, FG * NG)
            sp.dma_start(gain, io["ln2_g"].partition_broadcast(P)).then_inc(ln_loaded, 16)
            sp.dma_start(shift, io["ln2_b"].partition_broadcast(P)).then_inc(ln_loaded, 16)
            for t in range(NT):
                sp.wait_ge(ready[t % 2], t // 2 + 1)
                sp.dma_start(io["out"][P * t:P * t + P, :], acc[:, t, :]).then_inc(stored, 16)
            sp.wait_ge(stored, 16 * NT)

        @block.scalar
        def _(act):
            def split_up(g, f):
                act.wait_ge(u_loaded[f], 16 * g + 16)
                if not before(g, 1):
                    act.wait_ge(up_done, FG * g + (f - 1))
                act.activation(ups[0][:, f], uraw[:, f], ACT.Copy).then_inc(u_high, 1)

            def split_down(g, s, f):
                act.wait_ge(d_loaded[f], 16 * g + 16)
                if not before(g, 2):
                    act.wait_ge(dn_done, NT * g - NT)
                act.activation(dn[0][:, s, f, :], draw[:, f, :], ACT.Copy).then_inc(d_high, 1)

            def hidden(g, s, f):
                act.wait_ge(up_done, FG * g + (f + 1))
                if not before(g, 1):
                    act.wait_ge(s_low, FG * g + (f - 1))
                act.activation(hid[:, f, :].rearrange("p (b n) -> p b n", b=2), ps_u[:, f], ACT.Relu,
                               bias=bu[:, bass.ds(FG * g + f, 1)]).then_inc(rectified, 1)
                if not before(g, 2):
                    act.wait_ge(dn_done, NT * g - NT)
                act.wait_ge(rectified, FG * g + (f + 1))
                act.activation(hs[0][:, s, f, :], hid[:, f, :], ACT.Square).then_inc(s_high, 1)

            split_up(0, 0)
            split_up(0, 1)
            act.wait_ge(bu_loaded, 16)

            def turn(g, s):
                for f in range(FG):
                    split_down(g, s, f)
                for f in range(FG):
                    hidden(g, s, f)
                    if has_next(g, 1):
                        split_up(g + 1, f)
            loop(act, turn)
            for t in range(NT + 1):
                if t < NT:
                    act.wait_ge(var_ready, t + 1)
                    act.activation(sd[:, t:t + 1], var[:, t:t + 1], ACT.Sqrt).then_inc(sd_ready, 1)
                if t >= 1:
                    act.wait_ge(scale_ready, t)
                    act.activation(acc[:, t - 1, :], acc[:, t - 1, :], ACT.Identity, bias=bias[:, t - 1:t],
                                   scale=scale[:, t - 1:t]).then_inc(normalised, 1)

        @block.gpsimd
        def _(pool):
            pool.wait_ge(ln_loaded, 32)
            for t in range(NT):
                pool.wait_ge(normalised, t + 1)
                pool.tensor_tensor(acc[:, t, :], acc[:, t, :], gain, ALU.mult).then_inc(gained, 1)
                if t % 2 == 0:
                    pool.wait_ge(gained, t + 1)
                    pool.tensor_tensor(acc[:, t, :], acc[:, t, :], shift, ALU.add).then_inc(ready[0], 1)

        @block.vector
        def _(dve):
            dve.memset(eps[:, :], EPS)

            def split_up(g, f):
                dve.wait_ge(u_high, FG * g + (f + 1))
                dve.tensor_tensor(ups[1][:, f], uraw[:, f], f32(ups[0][:, f]), ALU.subtract).then_inc(u_low, 1)

            def split_down(g, s, f):
                dve.wait_ge(d_high, FG * g + (f + 1))
                dve.tensor_tensor(dn[1][:, s, f, :], draw[:, f, :], f32(dn[0][:, s, f, :]),
                                  ALU.subtract).then_inc(d_low, 1)

            def square(g, f):
                dve.wait_ge(s_high, FG * g + (f + 1))
                dve.tensor_tensor(hid[:, f, :], hid[:, f, :], hid[:, f, :], ALU.mult).then_inc(squared, 1)

            def square_low(g, s, f):
                dve.wait_ge(squared, FG * g + (f + 1))
                dve.tensor_tensor(hs[1][:, s, f, :], hid[:, f, :], f32(hs[0][:, s, f, :]),
                                  ALU.subtract).then_inc(s_low, 1)

            def add(g, t):
                dve.wait_ge(dn_done, NT * g + (t + 1))
                a2 = acc[:, t, :].rearrange("p (b n) -> p b n", b=2)
                dve.tensor_tensor(a2, a2, ps_d[:, t % 2], ALU.add).then_inc(added, 1)

            split_up(0, 0)
            split_up(0, 1)

            def turn(g, s):
                for f in range(FG):
                    split_down(g, s, f)
                square(g, 0)
                square_low(g, s, 0)
                if has_next(g, 1):
                    split_up(g + 1, 0)
                if not before(g, 1):
                    add(g - 1, 0)
                square(g, 1)
                square_low(g, s, 1)
                if not before(g, 1):
                    add(g - 1, 1)
                if has_next(g, 1):
                    split_up(g + 1, 1)
                if not before(g, 1):
                    for t in range(2, NT):
                        add(g - 1, t)
            loop(dve, turn)

            def statistics(t):
                dve.wait_ge(added, NT * (NG - 1) + (t + 1))
                for c in range(2):
                    dve.bn_stats(stats[:, t, c, :], acc[:, t, 512 * c:512 * c + 512])
                dve.drain()
                dve.bn_aggr(mv[:, t, :], stats[:, t, :, :])
                dve.drain()
                dve.tensor_tensor(var[:, t:t + 1], mv[:, t, 1:2], eps[:, :], ALU.add).then_inc(var_ready, 1)

            def scale_and_bias(t):
                c = slice(t, t + 1)
                dve.wait_ge(sd_ready, t + 1)
                refine_rsqrt(dve, var[:, c], sd[:, c], scale[:, c], tmp[:, c])
                dve.scalar_tensor_tensor(out=bias[:, c], in0=mv[:, t, 0:1], scalar=-1.0, in1=scale[:, c],
                                         op0=ALU.mult, op1=ALU.mult).then_inc(scale_ready, 1)

            def shift_tile(t):
                dve.wait_ge(gained, t + 1)
                dve.tensor_tensor(acc[:, t, :], acc[:, t, :], shift, ALU.add).then_inc(ready[1], 1)

            for t in range(NT + 2):
                if t < NT:
                    add(NG - 1, t)
                    statistics(t)
                if 1 <= t < NT + 1:
                    scale_and_bias(t - 1)
                if t >= 3 and t % 2:
                    shift_tile(t - 2)

        @block.tensor
        def _(pe):
            def up_half(g):
                for f in range(FG):
                    pe.wait_ge(u_low, FG * g + (f + 1))
                    if not before(g, 1):
                        pe.wait_ge(rectified, FG * g + (f - 1))
                    for c in range(KC):
                        for n_pass, (a, b) in enumerate(PASSES):
                            for q in range(2):
                                last = pe.matmul(ps_u[:, f, q, :], ups[a][:, f, c, :],
                                                 xT[b][:, c, 512 * q:512 * q + 512],
                                                 start=(c == 0 and n_pass == 0), stop=(c == KC - 1 and n_pass == 2))
                    last.then_inc(up_done, 1)

            def down_half(g, s):
                pe.wait_ge(s_low, FG * g + FG)
                pe.wait_ge(d_low, FG * g + FG)
                for t in range(NT):
                    if not (before(g, 1) and t < 2):
                        pe.wait_ge(added, NT * g + (t - 1))
                    for f in range(FG):
                        for n_pass, (a, b) in enumerate(PASSES):
                            for q in range(2):
                                last = pe.matmul(ps_d[:, t % 2, q, :], hs[a][:, s, f, P * t:P * t + P],
                                                 dn[b][:, s, f, 512 * q:512 * q + 512],
                                                 start=(f == 0 and n_pass == 0), stop=(f == FG - 1 and n_pass == 2))
                    last.then_inc(dn_done, 1)

            def turn(g, s):
                up_half(g)
                if not before(g, 1):
                    down_half(g - 1, 1 - s)
            loop(pe, turn)
            down_half(NG - 1, 1)


def build_program(nc, io):
    Kit.spent.clear()
    with Kit(nc, "all") as a:
        maskb = a.sb("maskb", [P, MB_LEN], BF16)
        ctok = [a.sb("ctok_high", [P, NT + 1, RANK], F32R), a.sb("ctok_low", [P, NT + 1, RANK], F32R)]
        cT = [a.sb("cT_high", [P, RC, T], F32R), a.sb("cT_low", [P, RC, T], F32R)]
        with Kit(nc, "hid") as h:
            hT = [h.sb("hT_high", [P, KC, T], F32R), h.sb("hT_low", [P, KC, T], F32R)]
            stage_norm(nc, io, hT)
            with Kit(nc, "sco") as s:
                scores = s.sb("scores", [P, SC_LEN])
                with Kit(nc, "kvq") as q:
                    kvq = q.sb("kvq", [P, N_KVQ, T])
                    stage_project_kvq(nc, io, hT, kvq)
                    kT2 = [q.sb("kT2_high", [P, T], F32R), q.sb("kT2_low", [P, T], F32R)]
                    widx = q.sb("widx", [P, NT, IDX_HEADS])
                    qs = q.sb("qs", [P, IDX_HEADS, S], F32R)
                    stage_keys(nc, io, kvq, ctok, cT, kT2, widx, qs)
                    stage_indexer(nc, qs, kT2, widx, scores)
                stage_project_select(nc, io, hT, scores, maskb)
        recycle(nc)
        stage_attention(nc, io, ctok, cT, maskb)
    recycle(nc)
    stage_recurrent(nc, io)
    with Kit(nc, "ffn") as f:
        mixed = [f.sb("mixed_high", [P, KC, S], F32R), f.sb("mixed_low", [P, KC, S], F32R)]
        stage_branch(nc, io, mixed)
        acc = f.sb("acc", [P, NT, D])
        stage_out(nc, io, mixed, acc)
        stage_mlp(nc, io, mixed, acc)


SCRATCH = {"h_tok": (NT, P, D), "projT": (N_PROJ, P, T), "oT": (HEADS, P, S), "yaT": (NB, P, S),
           "ybT": (KC, P, S)}


def layout(inputs):
    import numpy as np

    v = {n: np.asarray(a) for n, a in inputs.items()}
    w_in = v["w_in"][0].reshape(KC, P, -1).transpose(1, 0, 2)
    widths = (D_RNN, D_RNN, HEADS * P, RANK, IDX_HEADS * IDX_DIM, IDX_DIM, IDX_HEADS, D, D)
    start = [sum(widths[:n]) for n in range(len(widths))]

    def tiles(w, at, n):
        return [w[:, :, at + P * i:at + P * i + P] for i in range(n)]

    def column_tiles(w):
        w = w.reshape(w.shape[0] // P, P, w.shape[1]).transpose(1, 0, 2)
        return np.ascontiguousarray(np.stack(tiles(w, 0, w.shape[2] // P)))

    rest = [t for s, n in ((0, NB), (1, NB), (2, HEADS), (7, KC), (8, KC)) for t in tiles(w_in, start[s], n)]
    kvq = tiles(w_in, start[3], RC) + tiles(w_in, start[4], IDX_HEADS * IDX_DIM // P)
    kvq.append(np.zeros_like(kvq[0]))
    kvq[-1][:, :, 0:N_KW] = w_in[:, :, start[5]:start[7]]
    params = [v["conv_w"][0, t] for t in range(4)] + [v[n][0] for n in ("conv_b", "b_rg_a", "b_rg_x", "lru_lambda")]
    return {
        "x": v["x"][0], "meta_tokens": v["meta_tokens"],
        "ln_in_g": v["ln_in_g"], "ln_in_b": v["ln_in_b"], "kv_norm_g": v["kv_norm_g"][0],
        "ln1_g": v["ln1_g"][0], "ln1_b": v["ln1_b"][0], "ln2_g": v["ln2_g"][0], "ln2_b": v["ln2_b"][0],
        "b_down": v["b_down"][0],
        "w_kvq": np.stack(kvq), "w_rest": np.stack(rest),
        "w_uk": np.ascontiguousarray(v["w_uk"][0].transpose(2, 0, 1).reshape(P, HEADS * RANK)),
        "w_uv": np.ascontiguousarray(v["w_uv"][0].reshape(HEADS, RC, P, P).transpose(2, 1, 0, 3).reshape(P, -1)),
        "w_rg": np.ascontiguousarray(np.concatenate([v["w_rg_a"][0], v["w_rg_x"][0]], axis=2)),
        "lru_params": np.ascontiguousarray(np.stack(params).reshape(len(params), NB, P).transpose(2, 0, 1)),
        "w_branch_a": column_tiles(v["w_branch_a"][0]), "w_branch_b": column_tiles(v["w_branch_b"][0]),
        "w_out": v["w_out"][0], "w_up": column_tiles(v["w_up"][0]),
        "b_up": np.ascontiguousarray(v["b_up"][0].reshape(NF, P).transpose(1, 0)),
        "w_down": v["w_down"][0].reshape(NF, P, D),
    }


def kernel(**inputs):
    import numpy as np
    import concourse.bacc as bacc
    from concourse.bass_utils import run_bass_kernel_spmd

    nc = bacc.Bacc("TRN2", target_bir_lowering=False, num_devices=1)
    arrays, io = {}, {}
    for name, a in layout(inputs).items():
        arrays[f"in_{name}"] = np.ascontiguousarray(a)
        io[name] = nc.dram_tensor(f"in_{name}", a.shape, mybir.dt.from_np(a.dtype), kind="ExternalInput").ap()
    for name, shape in SCRATCH.items():
        io[name] = nc.dram_tensor(f"scratch_{name}", shape, F32, kind="Internal").ap()
    io["out"] = nc.dram_tensor("out_0", (S, D), F32, kind="ExternalOutput").ap()
    build_program(nc, io)
    r = run_bass_kernel_spmd(nc, [arrays], core_ids=[0])
    return r.results[0]["out_0"].reshape(1, S, D)
```
